# Optimizing a Trainium2 kernel written in Bass

```python
import jax, jax.numpy as jnp
from jax import lax
import numpy as np

D_MODEL = 1024
BATCH = 1
SEQ = 512
DEPTH = 2

CHUNK = 64
EPS = 1e-6
POOL_WINDOWS = (2, 4, 8, 16)
N_POOL_GROUPS = len(POOL_WINDOWS)
POOL_WIDTH = D_MODEL // 2
POOL_GROUP = POOL_WIDTH // N_POOL_GROUPS
HEAD_DIM = 64
N_Q_HEADS = 8
N_KV_HEADS = 2
GQ = N_Q_HEADS // N_KV_HEADS
Q_WIDTH = N_Q_HEADS * HEAD_DIM
KV_WIDTH = N_KV_HEADS * HEAD_DIM
WINDOW = 128
WINDOW_CHUNKS = WINDOW // CHUNK
ROPE_THETA = 10000.0
IN_WIDTH = POOL_WIDTH + Q_WIDTH + 2 * KV_WIDTH
N_BRANCHES = 2
D_FF = ((8 * D_MODEL // 3 + 255) // 256) * 256

kernel_name = "hybrid_pool_swa_sink_gated_block"

def rmsnorm(x, g):
    xf = x.astype(jnp.float32)
    y = xf * lax.rsqrt(jnp.mean(xf * xf, axis=-1, keepdims=True) + EPS)
    return (y * g.astype(jnp.float32)).astype(x.dtype)

def rope(t, pos):
    half = HEAD_DIM // 2
    freqs = ROPE_THETA ** (-jnp.arange(half, dtype=jnp.float32) / half)
    ang = pos.astype(jnp.float32)[:, None] * freqs[None, :]
    cos = jnp.cos(ang)[None, :, None, :]
    sin = jnp.sin(ang)[None, :, None, :]
    tf = t.astype(jnp.float32)
    t1, t2 = tf[..., :half], tf[..., half:]
    out = jnp.concatenate([t1 * cos - t2 * sin, t2 * cos + t1 * sin], axis=-1)
    return out.astype(t.dtype)

def multiscale_pool(u, w_group, scale):
    B, S, _ = u.shape
    uf = u.astype(jnp.float32).reshape(B, S, N_POOL_GROUPS, POOL_GROUP)
    c = jnp.pad(jnp.cumsum(uf, axis=1), ((0, 0), (1, 0), (0, 0), (0, 0)))
    t = jnp.arange(S)
    outs = []
    for g, w in enumerate(POOL_WINDOWS):
        start = jnp.maximum(t + 1 - w, 0)
        cg = c[:, :, g, :]
        total = cg[:, 1:] - jnp.take(cg, start, axis=1)
        cnt = (t + 1 - start).astype(jnp.float32)
        outs.append(total / cnt[None, :, None])
    pooled = jnp.stack(outs, axis=2) - uf
    y = jnp.einsum('bsgc,gcd->bsgd', pooled.astype(u.dtype), w_group)
    return y.reshape(B, S, POOL_WIDTH) * scale

def swa_sink_attention(q, k, v, sinks):
    B, S = q.shape[:2]
    n_chunks = S // CHUNK
    band_len = WINDOW_CHUNKS * CHUNK
    qc = q.reshape(B, n_chunks, CHUNK, N_KV_HEADS, GQ, HEAD_DIM)

    def band(t):
        tc = t.reshape(B, n_chunks, CHUNK, N_KV_HEADS, HEAD_DIM)
        tp = jnp.pad(tc, ((0, 0), (WINDOW_CHUNKS - 1, 0), (0, 0), (0, 0), (0, 0)))
        return jnp.concatenate([tp[:, i:i + n_chunks] for i in range(WINDOW_CHUNKS)], axis=2)

    kb, vb = band(k), band(v)
    s = jnp.einsum('bcqhgd,bckhd->bchgqk', qc, kb,
                   preferred_element_type=jnp.float32) * (HEAD_DIM ** -0.5)
    key_chunk = (jnp.arange(n_chunks)[:, None] - (WINDOW_CHUNKS - 1)
                 + jnp.arange(band_len)[None, :] // CHUNK)
    valid = (key_chunk >= 0)[None, :, None, None, None, :]
    s = jnp.where(valid, s, -jnp.inf)
    sink = sinks.astype(jnp.float32).reshape(N_KV_HEADS, GQ)[None, None, :, :, None, None]
    m = jnp.maximum(jnp.max(s, axis=-1, keepdims=True), sink)
    p = jnp.exp(s - m)
    p = p / (jnp.sum(p, axis=-1, keepdims=True) + jnp.exp(sink - m))
    o = jnp.einsum('bchgqk,bckhd->bcqhgd', p.astype(v.dtype), vb)
    return o.reshape(B, S, Q_WIDTH)

def setup_inputs(seed: int = 0) -> dict:
    key = jax.random.key(seed)
    ks = jax.random.split(key, 18)
    f32 = jnp.float32
    nrm = lambda k, shape, fan_in: jax.random.normal(k, shape, f32) * (fan_in ** -0.5)
    gain = lambda k, shape: 1.0 + 0.02 * jax.random.normal(k, shape, f32)
    return {
        "x": jax.random.normal(ks[0], (BATCH, SEQ, D_MODEL), f32),
        "norm_mix": gain(ks[1], (DEPTH, D_MODEL)),
        "w_in": nrm(ks[2], (DEPTH, D_MODEL, IN_WIDTH), D_MODEL),
        "pool_w": nrm(ks[3], (DEPTH, N_POOL_GROUPS, POOL_GROUP, POOL_GROUP), POOL_GROUP),
        "pool_scale": gain(ks[4], (DEPTH, POOL_WIDTH)),
        "w_branch_pool": nrm(ks[5], (DEPTH, POOL_WIDTH, D_MODEL), POOL_WIDTH),
        "w_branch_attn": nrm(ks[6], (DEPTH, Q_WIDTH, D_MODEL), Q_WIDTH),
        "sinks": 0.5 * jax.random.normal(ks[7], (DEPTH, N_Q_HEADS), f32),
        "w_gate": nrm(ks[8], (DEPTH, D_MODEL, N_BRANCHES * D_MODEL), D_MODEL),
        "b_gate": 0.01 * jax.random.normal(ks[9], (DEPTH, N_BRANCHES * D_MODEL), f32),
        "w_out": nrm(ks[10], (DEPTH, D_MODEL, D_MODEL), D_MODEL),
        "norm_ffn": gain(ks[11], (DEPTH, D_MODEL)),
        "w_ffn_gate": nrm(ks[12], (DEPTH, D_MODEL, D_FF), D_MODEL),
        "w_ffn_up": nrm(ks[13], (DEPTH, D_MODEL, D_FF), D_MODEL),
        "w_ffn_down": nrm(ks[14], (DEPTH, D_FF, D_MODEL), D_FF),
        "norm_final": gain(ks[15], (D_MODEL,)),
    }

def reference(x, norm_mix, w_in, pool_w, pool_scale, w_branch_pool, w_branch_attn, sinks,
              w_gate, b_gate, w_out, norm_ffn, w_ffn_gate, w_ffn_up, w_ffn_down, norm_final):
    B, S, _ = x.shape
    pos = jnp.arange(S)
    for l in range(DEPTH):
        h = rmsnorm(x, norm_mix[l])
        proj = h @ w_in[l]
        u = proj[..., :POOL_WIDTH]
        q = proj[..., POOL_WIDTH:POOL_WIDTH + Q_WIDTH].reshape(B, S, N_Q_HEADS, HEAD_DIM)
        k = proj[..., POOL_WIDTH + Q_WIDTH:POOL_WIDTH + Q_WIDTH + KV_WIDTH].reshape(
            B, S, N_KV_HEADS, HEAD_DIM)
        v = proj[..., POOL_WIDTH + Q_WIDTH + KV_WIDTH:].reshape(B, S, N_KV_HEADS, HEAD_DIM)
        a = multiscale_pool(u, pool_w[l], pool_scale[l]) @ w_branch_pool[l]
        q, k = rope(q, pos), rope(k, pos)
        b = swa_sink_attention(q, k, v, sinks[l]) @ w_branch_attn[l]
        gates = jax.nn.sigmoid(h @ w_gate[l] + b_gate[l])
        g_a, g_b = gates[..., :D_MODEL], gates[..., D_MODEL:]
        x = x + (g_a * a + g_b * b) @ w_out[l]
        h2 = rmsnorm(x, norm_ffn[l])
        x = x + (jax.nn.silu(h2 @ w_ffn_gate[l]) * (h2 @ w_ffn_up[l])) @ w_ffn_down[l]
    return rmsnorm(x, norm_final)


_drawn_inputs = setup_inputs


def setup_inputs(seed=0):
    import zlib

    import numpy as np

    out = dict(_drawn_inputs(seed))
    spreads = {}
    factors = {'norm_mix': 3.809,
     'pool_scale': 4.464,
     'sinks': 64.0,
     'b_gate': 8.0,
     'norm_ffn': 3.077,
     'norm_final': 8.195}
    for name, (base, spread) in spreads.items():
        noise = np.random.default_rng([zlib.crc32(name.encode()), seed]).standard_normal(out[name].shape)
        drawn = base * np.exp(spread * noise) if base else spread * noise
        out[name] = __import__('jax').numpy.asarray(drawn.astype(out[name].dtype))
    for name, factor in factors.items():
        out[name] = (out[name] * factor).astype(out[name].dtype)
    return out
```

```python
from contextlib import ExitStack

import concourse.bass as bass
from concourse import mybir

P = 128
D_MODEL, SEQ, DEPTH = 1024, 512, 2
CHUNK, HEAD_DIM, EPS = 64, 64, 1e-6
N_GROUPS, PAD = 4, 16
D_FF = 2816
KT = D_MODEL // P
HT = D_FF // P
TT = SEQ // P
STRIP = 2 * P
N_CHUNKS = SEQ // CHUNK
POOL_WIDTH, Q_WIDTH = 512, 512

F32 = mybir.dt.float32
F32R = mybir.dt.float32r
ALU = mybir.AluOpType
ACT = mybir.ActivationFunctionType
AX = mybir.AxisListType

N_U, N_KV, N_Q, N_G, N_POOL, N_G7 = 0, 2, 3, 5, 12, 13
N_BRANCH, N_OUT, N_FFN, N_DOWN = 14, 18, 22, 44
STRIPS = N_DOWN + 12
T_DOWN = N_DOWN
TURNS = T_DOWN + 4
DOWN_PARTS = (8, 8, 6)
WARM = 4
IN_ORDER = (0, 1, 4, 2, 3)
Y_BANKS = (0, 1, 4, 5)
LAST_ROWS = (0, 2, 3, 1)


def gate_strip(g):
    return N_G + g if g < 7 else N_G7


C_NEXT, C_FFN, C_BIAS, C_PSCALE, C_LAYER = 0, 8, 16, 32, 36
C_FIRST = DEPTH * C_LAYER
C_ALL = C_FIRST + KT


def trunk(nc, x, w_in, pool_w, w_branch_pool, w_branch_attn, w_gate, w_out, w_ffn_gate, w_ffn_up,
          w_ffn_down, vectors, sink_rows, tables, out):
    ctx = ExitStack()
    with ctx:
        top = [2048]

        def place(name, shape, dt, at=None):
            size = 4
            for s in shape[1:]:
                size *= s
            if at is None:
                at = top[0]
                top[0] += (size + 31) // 32 * 32
            return nc.alloc_sbuf_tensor_at(name, shape, dt, offset=at)

        xT = place("xT", [P, KT, SEQ], F32)
        n_hi = place("n_hi", [P, KT, SEQ], F32R)
        n_lo = place("n_lo", [P, KT, SEQ], F32R)
        raw = place("raw", [P, 2, KT, STRIP], F32)
        w_hi = place("w_hi", [P, 2, KT, STRIP], F32R)
        w_lo = place("w_lo", [P, 2, KT, STRIP], F32R)
        arena = top[0]
        top[0] += 98304
        gate = place("gate", [P, 2 * KT, SEQ], F32, arena)
        p_hi = place("p_hi", [P, N_GROUPS, SEQ], F32R, arena + 32768)
        p_lo = place("p_lo", [P, N_GROUPS, SEQ], F32R, arena + 40960)
        a_hi = place("a_hi", [P, 4, SEQ], F32R, arena + 49152)
        a_lo = place("a_lo", [P, 4, SEQ], F32R, arena + 57344)
        m_hi = place("m_hi", [P, KT, SEQ], F32R, arena + 65536)
        m_lo = place("m_lo", [P, KT, SEQ], F32R, arena + 81920)
        at = arena + 65536
        qT = place("qT", [P, 4, SEQ], F32, at)
        k_own = place("k_own", [P, SEQ], F32, at + 8192)
        k_swap = place("k_swap", [P, SEQ], F32, at + 10240)
        vT = place("vT", [P, SEQ], F32, at + 12288)
        v_win = place("v_win", [P, N_CHUNKS - 1, P], F32, at + 14336)
        u_pad = place("u_pad", [P, N_GROUPS, PAD + SEQ], F32, at + 17920)
        sum_a = place("sum_a", [P, PAD + SEQ], F32, at + 26368)
        sum_b = place("sum_b", [P, PAD + SEQ], F32, at + 28480)
        cos_r = place("cos_r", [P, SEQ], F32, arena + 49152)
        sin_r = place("sin_r", [P, SEQ], F32, arena + 51200)
        h_hi = place("h_hi", [P, HT, SEQ], F32R, arena)
        h_lo = place("h_lo", [P, HT, SEQ], F32R, arena + 45056)
        rows = place("rows", [P, TT, D_MODEL], F32, arena)

        tab = place("tab", [P, 2 * SEQ + P + N_GROUPS * PAD], F32)
        cos, sin = tab[:, 0:SEQ], tab[:, SEQ:2 * SEQ]
        ident = tab[:, 2 * SEQ:2 * SEQ + P]
        edge = tab[:, 2 * SEQ + P:].rearrange("p (g t) -> p g t", g=N_GROUPS)
        rstd = place("rstd", [P, SEQ], F32)
        sumsq = place("sumsq", [P, SEQ], F32)
        work = place("work", [P, 2, SEQ], F32)
        squares = place("squares", [P, 2, SEQ], F32)
        probs = place("probs", [P, 4, P], F32)
        probsT = place("probsT", [P, 4, P], F32)
        diag = place("diag", [P, TT, P], F32)
        ones = place("ones", [P, P], F32)
        ident_r = place("ident_r", [P, P], F32R)
        vec_rows = place("vec_rows", [C_ALL, P], F32)
        vec = place("vec", [P, C_ALL], F32)
        cur = place("cur", [P, C_LAYER], F32)
        sink_all = place("sink_all", [P, DEPTH, 4], F32)
        sink = place("sink", [P, 4], F32)
        ms = place("ms", [P, TT], F32)
        inv = place("inv", [P, TT], F32)
        rcol = place("rcol", [P, TT], F32)
        top_s = place("top_s", [P, 4], F32)
        peak = place("peak", [P, 4], F32)
        esink = place("esink", [P, 4], F32)
        total = place("total", [P, 4], F32)
        total_all = place("total_all", [P, 4], F32)
        inv_total = place("inv_total", [P, 4], F32)
        assert top[0] <= nc.sbuf_usable_end

        psum = ctx.enter_context(nc.psum_tensor("psum", [P, 8, SEQ], F32))
        B_S, B_PT, B_O = 4, 6, 7

        def main(t):
            return psum[:, 2 * (t % 2):2 * (t % 2) + 2, :]

        def side(t):
            return psum[:, 4 + 2 * (t % 2):6 + 2 * (t % 2), :]

        def sem(name):
            return ctx.enter_context(nc.semaphore(name))

        consts_in = sem("consts_in")
        rotary_in = sem("rotary_in")
        ident_ready = sem("ident_ready")
        vec_in = sem("vec_in")
        x_in = [sem(f"x_in{i}") for i in range(KT // 2)]
        sink_in = sem("sink_in")
        out_sent = sem("out_sent")
        raw_landed = [sem("raw_landed0"), sem("raw_landed1")]
        hi_ready = sem("hi_ready")
        lo_ready = sem("lo_ready")
        products = sem("products")
        evacuated = sem("evacuated")
        normed_hi = sem("normed_hi")
        normed_lo = sem("normed_lo")
        squared = sem("squared")
        summed = sem("summed")
        sum_half = sem("sum_half")
        col_sums = sem("col_sums")
        mean_sq = sem("mean_sq")
        inverse = sem("inverse")
        root = sem("root")
        diagonal = sem("diagonal")
        spread = sem("spread")
        rstd_ready = sem("rstd_ready")
        ones_ready = sem("ones_ready")
        vec_turned = sem("vec_turned")
        vec_ready = sem("vec_ready")
        cur_ready = sem("cur_ready")
        tables_scaled = sem("tables_scaled")
        rope_terms = sem("rope_terms")
        pads_clear = sem("pads_clear")
        pool_step = sem("pool_step")
        pooled = sem("pooled")
        pooled_hi = sem("pooled_hi")
        pooled_lo = sem("pooled_lo")
        y_hi = sem("y_hi")
        scores_done = sem("scores_done")
        softmax_step = sem("softmax_step")
        shifted = sem("shifted")
        exps_done = sem("exps_done")
        probs_ready = sem("probs_ready")
        probs_turned = sem("probs_turned")
        probsT_ready = sem("probsT_ready")
        heads_done = sem("heads_done")
        heads_hi = sem("heads_hi")
        heads_lo = sem("heads_lo")
        tanh_done = sem("tanh_done")
        mixed = sem("mixed")
        mix_hi = sem("mix_hi")
        mix_lo = sem("mix_lo")
        silu_done = sem("silu_done")
        hidden = sem("hidden")
        hid_hi = sem("hid_hi")
        hid_lo = sem("hid_lo")
        y_turned = sem("y_turned")
        y_dve = sem("y_dve")
        y_act = sem("y_act")
        v_turned = sem("v_turned")
        v_ready = sem("v_ready")

        def done(l, n):
            return l * STRIPS + (WARM + n + 1)

        def emptied(l, t):
            return l * TURNS + (WARM + t + 1)

        def bank_free(l, t):
            return emptied(l, t - 2)

        def slot_free(l, n):
            return done(l, n - 2)

        def split(l, n):
            return l * STRIPS + (n + 1)

        def raw_free(l, n):
            return split(l, n - 2)

        def landed(l, n):
            return l * (32 * (STRIPS // 2)) + 32 * (n // 2 + 1)

        x_cols = x[0].rearrange("(t p) (i c) -> i p t c", p=P, c=STRIP)

        def load_x(eng, i):
            eng.dma_start(rows[:, :, i * STRIP:(i + 1) * STRIP], x_cols[i]).then_inc(x_in[i], 16)

        block = ctx.enter_context(nc.Block())

        @block.sync
        def _(sp):
            def load(l, n, slot, first, second, wait=True):
                if wait:
                    sp.wait_ge(lo_ready, raw_free(l, n))
                for dst, src in (first, second):
                    sp.dma_start(raw[:, slot, dst[0]:dst[1], :], src).then_inc(raw_landed[slot], 16)

            def cols(w, l, c, k0=0, k1=KT, n_k=KT):
                v = w.rearrange("l (k p) m -> l p k m", p=P)
                return v[bass.ds(l, 1), :, k0:k1, bass.ds(c, STRIP)].rearrange("l p k m -> (l p) k m")

            def load_cols(l, n, slot, w, c, at=None, wait=True):
                at = l if at is None else at
                load(l, n, slot, ((0, 4), cols(w, at, c, 0, 4)), ((4, 8), cols(w, at, c, 4, 8)), wait)

            for i in (0, 2):
                load_x(sp, i)
            for n in range(2):
                load_cols(0, n, n, w_in, IN_ORDER[n] * STRIP, wait=False)
            with sp.Fori(0, DEPTH) as l:
                for n in range(2, 5):
                    load_cols(l, n, n % 2, w_in, IN_ORDER[n] * STRIP)
                for g in range(7):
                    load_cols(l, gate_strip(g), gate_strip(g) % 2, w_gate, g * STRIP)
                pw = pool_w.rearrange("l (k g) c d -> l c k g d", k=2)[bass.ds(l, 1)].rearrange(
                    "l c k g d -> (l c) k g d")
                sp.wait_ge(lo_ready, raw_free(l, N_POOL))
                for k in range(2):
                    sp.dma_start(raw[:, N_POOL % 2, k, :].rearrange("p (g d) -> p g d", g=2),
                                 pw[:, k]).then_inc(raw_landed[N_POOL % 2], 16)
                load_cols(l, N_G7, N_G7 % 2, w_gate, 7 * STRIP)
                with sp.Fori(0, 2) as i:
                    for s in range(2):
                        c = i * (2 * STRIP) + s * STRIP
                        load(l, i * 2 + (N_BRANCH + s), s,
                             ((0, 4), cols(w_branch_pool, l, c, 0, 4)),
                             ((4, 8), cols(w_branch_attn, l, c, 0, 4)))
                with sp.Fori(0, 2) as i:
                    for s in range(2):
                        load_cols(l, i * 2 + (N_OUT + s), s, w_out, i * (2 * STRIP) + s * STRIP)
                with sp.Fori(0, HT // 2) as j:
                    load_cols(l, j * 2 + N_FFN, 0, w_ffn_gate, j * STRIP)
                    load_cols(l, j * 2 + (N_FFN + 1), 1, w_ffn_up, j * STRIP)
                with sp.Fori(0, 2) as i:
                    for s in range(6):
                        c = i * (2 * STRIP) + (s // 3) * STRIP
                        k0 = sum(DOWN_PARTS[:s % 3])
                        nk = DOWN_PARTS[s % 3]
                        load(l, i * 6 + (N_DOWN + s), s % 2,
                             ((0, nk // 2), cols(w_ffn_down, l, c, k0, k0 + nk // 2)),
                             ((nk // 2, nk), cols(w_ffn_down, l, c, k0 + nk // 2, k0 + nk)))
                with sp.If(l < DEPTH - 1):
                    following = nc.s_assert_within(l + 1, 1, DEPTH - 1, skip_runtime_bounds_check_because=
                                                   "the If above holds only for layers before the last")
                    for n in range(2):
                        load_cols(l, STRIPS + n, n, w_in, IN_ORDER[n] * STRIP, at=following)
            for i, tt in enumerate(LAST_ROWS[0::2]):
                sp.wait_ge(y_dve, i + 1)
                sp.dma_start(out[0, tt * P:(tt + 1) * P, :], rows[:, tt, :]).then_inc(out_sent, 16)
            sp.wait_ge(out_sent, 16 * TT)

        @block.gpsimd
        def _(pool):
            def sum_squares(count, first, half):
                pool.wait_ge(squared, count)
                if first:
                    nc.gpsimd.tensor_tensor(sumsq[:], squares[:, 0, :], squares[:, 1, :],
                                            ALU.add).then_inc(summed, 1)
                else:
                    pool.wait_ge(summed, count - 1)
                    nc.gpsimd.tensor_tensor(sumsq[:], sumsq[:], squares[:, 0, :],
                                            ALU.add).then_inc(sum_half, 1)
                    pool.wait_ge(sum_half, half)
                    nc.gpsimd.tensor_tensor(sumsq[:], sumsq[:], squares[:, 1, :],
                                            ALU.add).then_inc(summed, 1)
            POOL_STEPS = sum(g + 1 for g in range(N_GROUPS)) + 2 * N_GROUPS

            for i in range(4):
                sum_squares(i + 1, i == 0, i)
            with pool.Fori(0, DEPTH) as l:
                pool.wait_ge(consts_in, 16)
                pool.wait_ge(pads_clear, l + 1)
                step = 0
                for g in range(N_GROUPS):
                    pool.wait_ge(evacuated, emptied(l, N_U + g // 2))
                    u = u_pad[:, g, :]
                    src, bufs = u, [sum_a, sum_b]
                    for e in range(g + 1):
                        d = 1 << e
                        dst = bufs[e % 2]
                        if e:
                            pool.wait_ge(pool_step, l * POOL_STEPS + step)
                        elif g:
                            pool.wait_ge(pooled, l * N_GROUPS + g)
                        nc.gpsimd.tensor_tensor(dst[:, 2 * d - 1:], src[:, 2 * d - 1:],
                                                src[:, d - 1:PAD + SEQ - d], ALU.add).then_inc(pool_step, 1)
                        step += 1
                        src = dst
                    mean = bufs[(g + 1) % 2]
                    pool.wait_ge(pool_step, l * POOL_STEPS + step)
                    nc.gpsimd.tensor_tensor(mean[:, PAD:2 * PAD], src[:, PAD:2 * PAD], edge[:, g, :],
                                            ALU.mult).then_inc(pool_step, 1)
                    nc.gpsimd.tensor_scalar(mean[:, 2 * PAD:], src[:, 2 * PAD:], 1.0 / (2 << g), 1.0,
                                            ALU.mult, ALU.mult).then_inc(pool_step, 1)
                    step += 2
                    pool.wait_ge(pool_step, l * POOL_STEPS + step)
                    nc.gpsimd.tensor_tensor(u[:, PAD:], mean[:, PAD:], u[:, PAD:],
                                            ALU.subtract).then_inc(pooled, 1)
                assert step == POOL_STEPS
                for i in range(8):
                    sum_squares(l * 8 + (4 + i + 1), i % 4 == 0, l * 6 + (3 + i - i // 4))

        @block.scalar
        def _(act):
            act.dma_start(tab[:, 2 * SEQ:], tables[:, 2 * SEQ:]).then_inc(consts_in, 16)
            act.dma_start(vec_rows[:], vectors).then_inc(vec_in, 16)
            for i in (1, 3):
                load_x(act, i)
            act.dma_start(tab[:, 0:2 * SEQ], tables[:, 0:2 * SEQ]).then_inc(rotary_in, 16)
            act.dma_start(sink_all[:], sink_rows).then_inc(sink_in, 16)

            def hi_split(l, n, slot, k=KT, j=0, wait=True):
                act.wait_ge(raw_landed[slot], landed(l, n) + 32 * j)
                if wait:
                    act.wait_ge(products, slot_free(l, n) + 2 * j)
                nc.scalar.activation(w_hi[:, slot, 0:k, :], raw[:, slot, 0:k, :], ACT.Copy).then_inc(hi_ready, 1)

            def norm_pair(i, count, ready, gain):
                act.wait_ge(evacuated, ready)
                if count is not None:
                    act.wait_ge(summed, count - 1)
                nc.scalar.activation(squares[:], xT[:, 2 * i:2 * i + 2, :], ACT.Square).then_inc(squared, 1)
                for m in (2 * i, 2 * i + 1):
                    nc.scalar.activation(n_hi[:, m, :], xT[:, m, :], ACT.Copy,
                                         scale=gain[:, m:m + 1]).then_inc(normed_hi, 1)

            def norm_root(count):
                act.wait_ge(inverse, count)
                nc.scalar.activation(rcol[:], inv[:], ACT.Sqrt).then_inc(root, 1)

            def norm_row(count):
                act.wait_ge(spread, count)
                nc.scalar.activation(rstd[:], psum[:, 5, :], ACT.Copy).then_inc(rstd_ready, 1)

            act.wait_ge(vec_ready, 2)
            for i in range(4):
                norm_pair(i, i + 1 if i else None, i + 1, vec[:, C_FIRST:])
                if i in (0, 3):
                    hi_split(0, i // 3, i // 3, wait=False)

            def gate_tanh(l, g):
                act.wait_ge(evacuated, emptied(l, gate_strip(g)))
                for m in (2 * g, 2 * g + 1):
                    nc.scalar.activation(gate[:, m, :], gate[:, m, :], ACT.Tanh, scale=0.5,
                                         bias=cur[:, C_BIAS + m:C_BIAS + m + 1]).then_inc(tanh_done, 1)

            def exps(l, c):
                w = P if c else CHUNK
                act.wait_ge(shifted, l * N_CHUNKS + (c + 1))
                nc.scalar.activation(probs[:, :, 0:w], probs[:, :, 0:w], ACT.Exp).then_inc(exps_done, 1)
                nc.scalar.activation(esink[:], esink[:], ACT.Exp).then_inc(exps_done, 1)

            def move_probsT(l, c):
                act.wait_ge(probs_turned, l * N_CHUNKS + (c + 1))
                nc.scalar.activation(probsT[:], psum[:, B_PT, :].rearrange("p (j r) -> p j r", j=4),
                                     ACT.Copy).then_inc(probsT_ready, 1)

            def move_heads(l, c):
                act.wait_ge(heads_done, l * N_CHUNKS + (c + 1))
                nc.scalar.activation(a_hi[:, :, c * CHUNK:(c + 1) * CHUNK],
                                     psum[:, B_O, 0:4 * CHUNK].rearrange("p (j q) -> p j q", j=4),
                                     ACT.Copy).then_inc(heads_hi, 1)

            def mix_pair(l, i):
                act.wait_ge(mixed, l * 4 + (i + 1))
                nc.scalar.activation(m_hi[:, 2 * i:2 * i + 2, :], work[:], ACT.Copy).then_inc(mix_hi, 1)

            def ffn_gate(l, j):
                act.wait_ge(evacuated, emptied(l, N_FFN) + 2 * j)
                nc.scalar.activation(work[:], work[:], ACT.Silu).then_inc(silu_done, 1)

            def ffn_hidden(l, j, count):
                act.wait_ge(hidden, count)
                nc.scalar.activation(h_hi[:, bass.ds(j * 2, 2), :], squares[:], ACT.Copy).then_inc(hid_hi, 1)

            with act.Fori(0, DEPTH) as l:
                act.wait_ge(cur_ready, l * 2 + 2)
                norm_root(l * 2 + 1)
                hi_split(l, 2, 0)
                norm_row(l * 2 + 1)
                for n in range(3, 6):
                    hi_split(l, n, n % 2)
                for w in range(8):
                    if w == 7:
                        hi_split(l, N_G7, N_G7 % 2)
                        for g in range(N_GROUPS):
                            act.wait_ge(products, done(l, N_POOL))
                            nc.scalar.activation(p_hi[:, g, :], psum[:, Y_BANKS[g], :], ACT.Copy,
                                                 scale=cur[:, C_PSCALE + g:C_PSCALE + g + 1]).then_inc(y_hi, 1)
                    if w:
                        move_probsT(l, w - 1)
                    if w < 7:
                        n = gate_strip(w) + 1
                        hi_split(l, n, n % 2, KT if n != N_POOL else 2)
                    if w == 5:
                        act.wait_ge(pooled, l * N_GROUPS + N_GROUPS)
                        nc.scalar.activation(p_hi[:], u_pad[:, :, PAD:], ACT.Copy).then_inc(pooled_hi, 1)
                    if w:
                        gate_tanh(l, w - 1)
                    exps(l, w)
                    if w:
                        move_heads(l, w - 1)
                    if w == 7:
                        hi_split(l, N_BRANCH, 0)
                move_probsT(l, 7)
                hi_split(l, N_BRANCH + 1, 1)
                gate_tanh(l, 7)
                move_heads(l, 7)
                for i in range(4):
                    n = N_BRANCH + 2 + i
                    if i < 3:
                        hi_split(l, n, n % 2)
                        mix_pair(l, i)
                    else:
                        mix_pair(l, i)
                        hi_split(l, n, n % 2)
                for i in range(4):
                    norm_pair(i, l * 8 + (4 + i + 1), emptied(l, N_OUT + i), cur[:, C_FFN:])
                    n = N_OUT + 2 + i
                    hi_split(l, n, n % 2)
                norm_root(l * 2 + 2)
                hi_split(l, N_FFN + 2, 0)
                norm_row(l * 2 + 2)
                ffn_gate(l, 0)
                with act.Fori(1, HT // 2) as j:
                    ffn_hidden(l, j - 1, l * (HT // 2) + j)
                    hi_split(l, N_FFN + 1, 1, j=j)
                    ffn_gate(l, j)
                    hi_split(l, N_FFN + 2, 0, j=j)
                ffn_hidden(l, HT // 2 - 1, l * (HT // 2) + HT // 2)
                for n in range(N_DOWN + 1, STRIPS):
                    i, r = divmod(n - 1 - N_DOWN, 3)
                    if r == 0 and i:
                        norm_pair(i - 1, l * 8 + (8 + i), emptied(l, T_DOWN + i - 1), cur[:, C_NEXT:])
                    hi_split(l, n, n % 2, DOWN_PARTS[(n - N_DOWN) % 3])
                with act.If(l < DEPTH - 1):
                    hi_split(l, STRIPS, 0)
                norm_pair(3, l * 8 + 12, emptied(l, T_DOWN + 3), cur[:, C_NEXT:])
                with act.If(l < DEPTH - 1):
                    hi_split(l, STRIPS + 1, 1)

            norm_root(2 * DEPTH + 1)
            act.wait_ge(root, 2 * DEPTH + 1)
            for i, tt in ((1, LAST_ROWS[1]), (3, LAST_ROWS[3])):
                act.wait_ge(y_turned, i + 1)
                nc.scalar.activation(rows[:, tt, :], psum[:, 2 * tt:2 * tt + 2, :].rearrange("p a b -> p (a b)"),
                                     ACT.Copy, scale=rcol[:, tt:tt + 1]).then_inc(y_act, 1)
            for i, tt in enumerate(LAST_ROWS[1::2]):
                act.wait_ge(y_act, i + 1)
                act.dma_start(out[0, tt * P:(tt + 1) * P, :], rows[:, tt, :]).then_inc(out_sent, 16)

        @block.tensor
        def _(pe):
            def three(bank, slot, k, m, hi, lo, start, stop):
                c = slice(m * P, (m + 1) * P)
                nc.tensor.matmul(bank, w_lo[:, slot, k, c], hi, start=start, stop=False)
                nc.tensor.matmul(bank, w_hi[:, slot, k, c], lo, start=False, stop=False)
                return nc.tensor.matmul(bank, w_hi[:, slot, k, c], hi, start=False, stop=stop)

            def strip(slot, banks, hi, lo, k0=0, k1=KT, r0=0, before=None, first=True, last=True, end=True):
                for k in range(k0, k1):
                    if before and k in before:
                        before[k]()
                    for m in range(2):
                        mm = three(banks[:, m, :], slot, k, m, hi[:, r0 + k - k0, :], lo[:, r0 + k - k0, :],
                                   first and k == k0, last and k == k1 - 1)
                if end:
                    mm.then_inc(products, 1)

            def ready(l, n, t=None):
                pe.wait_ge(lo_ready, split(l, n))
                if t is not None:
                    pe.wait_ge(evacuated, bank_free(l, t))

            def column_sums(sums, bank=4):
                pe.wait_ge(summed, sums)
                for tt in range(TT):
                    mm = nc.tensor.matmul(psum[:, bank, tt:tt + 1], sumsq[:, tt * P:(tt + 1) * P],
                                          ones[:, 0:1], start=True, stop=True)
                mm.then_inc(col_sums, 1)

            def spread_rstd(count):
                pe.wait_ge(diagonal, count)
                nc.tensor.matmul(psum[:, 5, :], ones[:], diag[:].rearrange("p a b -> p (a b)"), start=True,
                                 stop=True).then_inc(spread, 1)

            def scores_wait(l, c):
                if c == 0:
                    pe.wait_ge(evacuated, emptied(l, N_Q + 1))
                if c == N_CHUNKS - 1:
                    pe.wait_ge(evacuated, emptied(l, N_POOL))
                if c >= 2:
                    pe.wait_ge(shifted, l * N_CHUNKS + (c - 1))

            def scores(l, c):
                k0 = max(c - 1, 0) * CHUNK
                w = (c + 1) * CHUNK - k0
                for j in range(4):
                    for h in range(2):
                        part = slice(h * CHUNK, (h + 1) * CHUNK)
                        keys = k_own if j // 2 == h else k_swap
                        mm = nc.tensor.matmul(psum[part, B_S + c % 2, j * P:j * P + w],
                                              qT[part, j, c * CHUNK:(c + 1) * CHUNK],
                                              keys[part, k0:k0 + w], start=True, stop=True)
                mm.then_inc(scores_done, 1)

            def turn_probs(l, c):
                pe.wait_ge(probs_ready, l * N_CHUNKS + (c + 1))
                if c == 0:
                    pe.wait_ge(v_ready, l + 1)
                for j in range(4):
                    mm = nc.tensor.transpose(psum[:, B_PT, j * P:(j + 1) * P], probs[:, j, :], ident)
                mm.then_inc(probs_turned, 1)

            def heads_wait(l, c):
                pe.wait_ge(probsT_ready, l * N_CHUNKS + (c + 1))
                if c:
                    pe.wait_ge(heads_lo, l * N_CHUNKS + c)

            def heads(l, c):
                keys = slice(0, P if c else CHUNK)
                win = max(c - 1, 0)
                for g in range(2):
                    for h in range(2):
                        o = psum[h * HEAD_DIM:(h + 1) * HEAD_DIM, B_O, g * P:(g + 1) * P]
                        mm = nc.tensor.matmul(o.rearrange("p (j q) -> p j q", j=2),
                                              v_win[keys, win, g * HEAD_DIM:(g + 1) * HEAD_DIM],
                                              probsT[keys, 2 * g:2 * g + 2, h * CHUNK:(h + 1) * CHUNK],
                                              start=True, stop=True)
                mm.then_inc(heads_done, 1)

            pe.wait_ge(consts_in, 16)
            pe.wait_ge(vec_in, 16)
            nc.tensor.transpose(psum[:, 7, 0:C_ALL], vec_rows[:], ident[0:C_ALL, 0:C_ALL]).then_inc(vec_turned, 1)
            for m in range(KT):
                if m % 2 == 0:
                    pe.wait_ge(x_in[m // 2], 16)
                if m == KT - 1:
                    pe.wait_ge(vec_ready, 1)
                for tt in range(TT):
                    mm = nc.tensor.transpose(psum[:, m, tt * P:(tt + 1) * P], rows[:, tt, m * P:(m + 1) * P],
                                             ident)
                if m % 2:
                    mm.then_inc(products, 1)
            pe.wait_ge(ones_ready, 2)

            with pe.Fori(0, DEPTH) as l:
                def normed(base):
                    return {2 * i: (lambda i=i: pe.wait_ge(normed_lo, l * 8 + (base + i + 1)))
                            for i in range(4)}

                ready(l, 0, 0)
                strip(0, main(0), n_hi, n_lo, before=normed(0))
                column_sums(l * 8 + 4)
                ready(l, 1, 1)
                strip(1, main(1), n_hi, n_lo, before={5: lambda: spread_rstd(l * 2 + 1)})
                for n in range(2, N_G):
                    ready(l, n, n)
                    strip(n % 2, main(n), n_hi, n_lo)
                for w in range(8):
                    before = {}
                    if w:
                        before[2] = lambda c=w - 1: turn_probs(l, c)
                        before[5] = lambda c=w - 1: heads_wait(l, c)
                        before[6] = lambda c=w - 1: heads(l, c)
                        before[4] = lambda c=w: scores(l, c)
                    before[7 if w == 0 else 3] = lambda c=w: scores_wait(l, c)
                    if w == 7:
                        ready(l, N_POOL, N_POOL)
                        pe.wait_ge(pooled_lo, l + 1)
                        pe.wait_ge(shifted, l * N_CHUNKS + 7)
                        for g in range(N_GROUPS):
                            mm = three(psum[:, Y_BANKS[g], :], N_POOL % 2, g // 2, g % 2, p_hi[:, g, :],
                                       p_lo[:, g, :], True, True)
                        mm.then_inc(products, 1)
                    n = gate_strip(w)
                    ready(l, n, n)
                    strip(n % 2, main(n), n_hi, n_lo, before=before)
                    if w == 0:
                        scores(l, 0)
                        for i in range(N_CHUNKS - 1):
                            mm = nc.tensor.transpose(psum[:, B_PT + i // 4, (i % 4) * P:(i % 4 + 1) * P],
                                                     vT[:, i * CHUNK:i * CHUNK + P], ident)
                        mm.then_inc(v_turned, 1)
                for i in range(4):
                    n = N_BRANCH + i
                    ready(l, n, n)
                    before = {1: lambda: turn_probs(l, 7), 2: lambda: heads_wait(l, 7),
                              3: lambda: heads(l, 7)} if i == 0 else None
                    strip(n % 2, main(n), p_hi, p_lo, 0, 4, before=before, end=False)
                    if i == 0:
                        pe.wait_ge(heads_lo, l * N_CHUNKS + N_CHUNKS)
                    strip(n % 2, side(n), a_hi, a_lo, 4, 8)
                with pe.Fori(0, 2) as i:
                    for s in range(2):
                        pe.wait_ge(lo_ready, split(l, N_OUT + s) + 2 * i)
                        pe.wait_ge(evacuated, bank_free(l, N_OUT + s) + 2 * i)
                        before = {2 * q: (lambda q=q: pe.wait_ge(mix_lo, l * 4 + (q + 1))) for q in range(4)}
                        strip(s, main(s), m_hi, m_lo, before=before)

                def ffn(j, stats=None):
                    for s in range(2):
                        pe.wait_ge(lo_ready, split(l, N_FFN + s) + 2 * j)
                        pe.wait_ge(evacuated, bank_free(l, N_FFN + s) + 2 * j)
                        before = None
                        if stats:
                            before = normed(4) if s == 0 else {5: lambda: spread_rstd(l * 2 + 2)}
                        strip(s, main(s), n_hi, n_lo, before=before)
                        if stats and s == 0:
                            column_sums(l * 8 + 8)

                ffn(0, True)
                with pe.Fori(1, HT // 2) as j:
                    ffn(j)
                with pe.Fori(0, 2) as i:
                    for s in range(6):
                        r = s % 3
                        pe.wait_ge(lo_ready, split(l, N_DOWN + s) + 6 * i)
                        if r == 0:
                            pe.wait_ge(evacuated, bank_free(l, T_DOWN + s // 3) + 2 * i)
                        if r < 2:
                            pe.wait_ge(hid_lo, l * (HT // 2) + 4 * (r + 1))
                            before = None
                        else:
                            pe.wait_ge(hid_lo, l * (HT // 2) + (HT // 2 - 1))
                            before = {DOWN_PARTS[2] - 2: lambda: pe.wait_ge(hid_lo, l * (HT // 2) + HT // 2)}
                        strip(s % 2, main(s // 3), h_hi, h_lo, 0, DOWN_PARTS[r], sum(DOWN_PARTS[:r]),
                              before=before, first=r == 0, last=r == 2)

            pe.wait_ge(ident_ready, 1)
            def turn_x(tt, m):
                o = psum[:, 2 * tt + m // 4, (m % 4) * P:(m % 4 + 1) * P]
                c = slice(tt * P, (tt + 1) * P)
                nc.tensor.matmul(o, n_lo[:, m, c], ident_r[:], start=True, stop=False)
                return nc.tensor.matmul(o, n_hi[:, m, c], ident_r[:], start=False, stop=True)
            for m in range(KT):
                if m % 2 == 0:
                    pe.wait_ge(normed_lo, 8 * DEPTH + m // 2 + 1)
                for tt in LAST_ROWS[:-1]:
                    mm = turn_x(tt, m)
                    if m == KT - 1:
                        mm.then_inc(y_turned, 1)
            column_sums(8 * DEPTH + 4, 2 * LAST_ROWS[-1])
            pe.wait_ge(mean_sq, 2 * DEPTH + 1)
            for m in range(KT):
                mm = turn_x(LAST_ROWS[-1], m)
            mm.then_inc(y_turned, 1)

        @block.vector
        def _(dve):
            nc.vector.memset(ones[:], 1.0).then_inc(ones_ready, 1)
            nc.vector.memset(probs[:], 0.0).then_inc(ones_ready, 1)

            def lo_split(l, n, slot, k=KT, j=0):
                dve.wait_ge(hi_ready, l * STRIPS + (n + 1) + 2 * j)
                nc.vector.tensor_tensor(w_lo[:, slot, 0:k, :], raw[:, slot, 0:k, :],
                                        w_hi[:, slot, 0:k, :].bitcast(F32), ALU.subtract).then_inc(lo_ready, 1)

            def norm_pair(i, count, gain):
                for m in (2 * i, 2 * i + 1):
                    dve.wait_ge(normed_hi, count * 2 - (2 * i + 1 - m))
                    mm = nc.vector.scalar_tensor_tensor(n_lo[:, m, :], xT[:, m, :], gain[:, m:m + 1],
                                                        n_hi[:, m, :].bitcast(F32), ALU.mult, ALU.subtract)
                mm.then_inc(normed_lo, 1)

            def norm_columns(count, bank=4):
                dve.wait_ge(col_sums, count)
                nc.vector.tensor_scalar(ms[:], psum[:, bank, 0:TT], 1.0 / D_MODEL, EPS, ALU.mult,
                                        ALU.add).then_inc(mean_sq, 1)
                dve.wait_ge(mean_sq, count)
                nc.vector.reciprocal(inv[:], ms[:]).then_inc(inverse, 1)

            def norm_diagonal(count):
                dve.wait_ge(root, count)
                nc.vector.tensor_tensor(diag[:], ident.unsqueeze(1).to_broadcast([P, TT, P]),
                                        rcol[:].unsqueeze(2).to_broadcast([P, TT, P]),
                                        ALU.mult).then_inc(diagonal, 1)

            def pair(ap):
                return ap.unsqueeze(1).to_broadcast([P, 2, SEQ])

            dve.wait_ge(vec_turned, 1)
            nc.vector.tensor_copy(vec[:], psum[:, 7, 0:C_ALL]).then_inc(vec_ready, 1)
            dve.wait_ge(vec_ready, 1)
            bias = vec[:, 0:C_FIRST].rearrange("p (l c) -> p l c", l=DEPTH)[:, :, C_BIAS:C_PSCALE]
            nc.vector.tensor_scalar(bias, bias, 0.5, None, ALU.mult).then_inc(vec_ready, 1)
            for i in range(4):
                dve.wait_ge(products, i + 1)
                nc.vector.tensor_copy(xT[:, 2 * i:2 * i + 2, :], psum[:, 2 * i:2 * i + 2, :]).then_inc(evacuated, 1)
                dve.wait_ge(evacuated, i + 1)
                norm_pair(i, i + 1, vec[:, C_FIRST:])
                if i in (0, 3):
                    lo_split(0, i // 3, i // 3)
            dve.wait_ge(consts_in, 16)
            nc.vector.tensor_copy(ident_r[:], ident).then_inc(ident_ready, 1)
            dve.wait_ge(rotary_in, 16)
            dve.wait_ge(sink_in, 16)
            dve.wait_ge(vec_ready, 2)

            def rotate(l, t, n_rot, dsts, count):
                src = main(t)[:, 0:n_rot, :]
                by = [P, n_rot, SEQ]
                if t > N_KV:
                    dve.wait_ge(evacuated, emptied(l, t - 1))
                nc.vector.tensor_tensor(work[:, 0:n_rot, :], src, cos_r[:].unsqueeze(1).to_broadcast(by), ALU.mult)
                for q in range(4):
                    a, b = q * 32, (q ^ 1) * 32
                    mm = nc.vector.tensor_tensor(
                        squares[a:a + 32, 0:n_rot, :], src[b:b + 32],
                        sin_r[b:b + 32, :].unsqueeze(1).to_broadcast([32, n_rot, SEQ]), ALU.mult)
                mm.then_inc(rope_terms, 1)
                dve.wait_ge(rope_terms, count)
                for dst, part in dsts:
                    mm = nc.vector.tensor_tensor(dst, work[part, 0:n_rot, :], squares[part, 0:n_rot, :], ALU.add)
                return mm

            STEPS = 5

            def shift_scores(l, c):
                w = P if c else CHUNK
                s = psum[:, B_S + c % 2, :].rearrange("p (j k) -> p j k", j=4)[:, :, 0:w]
                at = l * (STEPS * N_CHUNKS) + STEPS * c
                dve.wait_ge(scores_done, l * N_CHUNKS + (c + 1))
                nc.vector.tensor_reduce(top_s[:], s, AX.X, ALU.max).then_inc(softmax_step, 1)
                dve.wait_ge(softmax_step, at + 1)
                nc.vector.scalar_tensor_tensor(peak[:], top_s[:], HEAD_DIM ** -0.5, sink[:], ALU.mult,
                                               ALU.max).then_inc(softmax_step, 1)
                dve.wait_ge(softmax_step, at + 2)
                nc.vector.tensor_tensor(esink[:], sink[:], peak[:], ALU.subtract)
                if c:
                    dve.wait_ge(probs_turned, l * N_CHUNKS + c)
                nc.vector.scalar_tensor_tensor(probs[:, :, 0:w], s, HEAD_DIM ** -0.5,
                                               peak[:].unsqueeze(2).to_broadcast([P, 4, w]), ALU.mult,
                                               ALU.subtract).then_inc(shifted, 1)

            def normalise(l, c):
                w = P if c else CHUNK
                at = l * (STEPS * N_CHUNKS) + STEPS * c
                dve.wait_ge(exps_done, l * (2 * N_CHUNKS) + 2 * (c + 1))
                nc.vector.tensor_reduce(total[:], probs[:, :, 0:w], AX.X, ALU.add).then_inc(softmax_step, 1)
                dve.wait_ge(softmax_step, at + 3)
                nc.vector.tensor_tensor(total_all[:], total[:], esink[:], ALU.add).then_inc(softmax_step, 1)
                dve.wait_ge(softmax_step, at + 4)
                nc.vector.reciprocal(inv_total[:], total_all[:]).then_inc(softmax_step, 1)
                dve.wait_ge(softmax_step, at + 5)
                nc.vector.tensor_tensor(probs[:, :, 0:w], probs[:, :, 0:w],
                                        inv_total[:].unsqueeze(2).to_broadcast([P, 4, w]),
                                        ALU.mult).then_inc(probs_ready, 1)

            def move_heads(l, c):
                dve.wait_ge(heads_hi, l * N_CHUNKS + (c + 1))
                cols = slice(c * CHUNK, (c + 1) * CHUNK)
                nc.vector.tensor_tensor(a_lo[:, :, cols],
                                        psum[:, B_O, 0:4 * CHUNK].rearrange("p (j q) -> p j q", j=4),
                                        a_hi[:, :, cols].bitcast(F32), ALU.subtract).then_inc(heads_lo, 1)

            def scaled(l, t, dst):
                dve.wait_ge(products, done(l, t))
                nc.vector.tensor_tensor(dst, main(t), pair(rstd[:]), ALU.mult).then_inc(evacuated, 1)

            def mix_pair(l, i):
                t = N_BRANCH + i
                if i == 0:
                    dve.wait_ge(tanh_done, l * 16 + 16)
                else:
                    dve.wait_ge(mix_lo, l * 4 + i)
                dve.wait_ge(products, done(l, t))
                nc.vector.scalar_tensor_tensor(work[:], gate[:, 2 * i:2 * i + 2, :], 1.0, main(t), ALU.add,
                                               ALU.mult)
                nc.vector.scalar_tensor_tensor(squares[:], gate[:, KT + 2 * i:KT + 2 * i + 2, :], 1.0,
                                               side(t), ALU.add, ALU.mult).then_inc(evacuated, 1)
                dve.wait_ge(evacuated, emptied(l, t))
                nc.vector.tensor_tensor(work[:], work[:], squares[:], ALU.add).then_inc(mixed, 1)
                dve.wait_ge(mix_hi, l * 4 + (i + 1))
                dve.wait_ge(mixed, l * 4 + (i + 1))
                nc.vector.tensor_tensor(m_lo[:, 2 * i:2 * i + 2, :], work[:],
                                        m_hi[:, 2 * i:2 * i + 2, :].bitcast(F32), ALU.subtract).then_inc(mix_lo, 1)

            def residual(l, i, t, n, factor, count, gain):
                dve.wait_ge(products, done(l, n))
                tiles = xT[:, 2 * i:2 * i + 2, :]
                nc.vector.scalar_tensor_tensor(tiles, main(t), factor, tiles, ALU.mult,
                                               ALU.add).then_inc(evacuated, 1)
                dve.wait_ge(evacuated, emptied(l, t))
                norm_pair(i, count, gain)

            def ffn_gate(l, j):
                dve.wait_ge(products, done(l, N_FFN) + 2 * j)
                nc.vector.tensor_tensor(work[:], main(N_FFN), pair(rstd[:]), ALU.mult).then_inc(evacuated, 1)

            def ffn_hidden(l, j, count):
                dve.wait_ge(lo_ready, split(l, N_FFN + 2) + 2 * j)
                dve.wait_ge(products, done(l, N_FFN + 1) + 2 * j)
                nc.vector.tensor_tensor(squares[:], main(N_FFN + 1), pair(rstd[:]), ALU.mult).then_inc(evacuated, 1)
                dve.wait_ge(evacuated, emptied(l, N_FFN + 1) + 2 * j)
                dve.wait_ge(silu_done, count)
                nc.vector.tensor_tensor(squares[:], squares[:], work[:], ALU.mult).then_inc(hidden, 1)
                dve.wait_ge(hidden, count)
                dve.wait_ge(hid_hi, count)
                tiles = bass.ds(j * 2, 2)
                nc.vector.tensor_tensor(h_lo[:, tiles, :], squares[:], h_hi[:, tiles, :].bitcast(F32),
                                        ALU.subtract).then_inc(hid_lo, 1)

            with dve.Fori(0, DEPTH) as l:
                dve.wait_ge(normed_lo, l * 8 + 4)
                nc.vector.tensor_copy(cur[:], vec[:, bass.ds(l * C_LAYER, C_LAYER)]).then_inc(cur_ready, 1)
                nc.vector.tensor_copy(sink[:], sink_all[:, bass.ds(l, 1), :].rearrange("p a j -> p (a j)")
                                      ).then_inc(cur_ready, 1)
                nc.vector.memset(u_pad[:, :, 0:PAD], 0.0).then_inc(pads_clear, 1)
                dve.wait_ge(cur_ready, l * 2 + 2)
                norm_columns(l * 2 + 1)
                norm_diagonal(l * 2 + 1)
                lo_split(l, 2, 0)
                dve.wait_ge(rstd_ready, l * 2 + 1)
                scaled(l, N_U, u_pad[:, 0:2, PAD:])
                nc.vector.tensor_tensor(cos_r[:], cos, rstd[:], ALU.mult)
                nc.vector.tensor_tensor(sin_r[:], sin, rstd[:], ALU.mult).then_inc(tables_scaled, 1)
                lo_split(l, 3, 1)
                scaled(l, N_U + 1, u_pad[:, 2:4, PAD:])
                lo_split(l, 4, 0)
                dve.wait_ge(tables_scaled, l + 1)
                dve.wait_ge(products, done(l, N_KV))
                nc.vector.tensor_tensor(vT[:], main(N_KV)[:, 1, :], rstd[:], ALU.mult)
                lower, upper = slice(0, HEAD_DIM), slice(HEAD_DIM, P)
                rotate(l, N_KV, 1, [(k_own[:].unsqueeze(1), slice(0, P)),
                                    (k_swap[upper, :].unsqueeze(1), lower),
                                    (k_swap[lower, :].unsqueeze(1), upper)],
                       l * 3 + 1).then_inc(evacuated, 1)
                lo_split(l, 5, 1)
                dve.wait_ge(products, done(l, N_Q))
                rotate(l, N_Q, 2, [(qT[:, 0:2, :], slice(0, P))], l * 3 + 2).then_inc(evacuated, 1)
                for w in range(8):
                    def split_next():
                        if w < 7:
                            n = gate_strip(w) + 1
                            lo_split(l, n, n % 2, KT if n != N_POOL else 2)
                        else:
                            lo_split(l, N_G7, N_G7 % 2)
                    if w == 0:
                        split_next()
                        dve.wait_ge(products, done(l, N_Q + 1))
                        rotate(l, N_Q + 1, 2, [(qT[:, 2:4, :], slice(0, P))], l * 3 + 3).then_inc(evacuated, 1)
                    else:
                        g = w - 1
                        if w == 1:
                            dve.wait_ge(v_turned, l + 1)
                            flat = psum[:, B_PT:B_O + 1, :].rearrange("p a b -> p (a b)")[:, 0:(N_CHUNKS - 1) * P]
                            nc.vector.tensor_copy(v_win[:].rearrange("p a b -> p (a b)"), flat).then_inc(v_ready, 1)
                        scaled(l, gate_strip(g), gate[:, 2 * g:2 * g + 2, :])
                        split_next()
                    if w == 7:
                        for g in range(N_GROUPS):
                            dve.wait_ge(y_hi, l * N_GROUPS + (g + 1))
                            mm = nc.vector.scalar_tensor_tensor(p_lo[:, g, :], psum[:, Y_BANKS[g], :],
                                                                cur[:, C_PSCALE + g:C_PSCALE + g + 1],
                                                                p_hi[:, g, :].bitcast(F32), ALU.mult, ALU.subtract)
                        mm.then_inc(evacuated, 1)
                    if w == 5:
                        dve.wait_ge(pooled_hi, l + 1)
                        nc.vector.tensor_tensor(p_lo[:], u_pad[:, :, PAD:], p_hi[:].bitcast(F32),
                                                ALU.subtract).then_inc(pooled_lo, 1)
                    shift_scores(l, w)
                    normalise(l, w)
                    if w:
                        move_heads(l, w - 1)
                    if w == 7:
                        lo_split(l, N_BRANCH, 0)
                scaled(l, N_G7, gate[:, 14:16, :])
                lo_split(l, N_BRANCH + 1, 1)
                move_heads(l, 7)
                for i in range(4):
                    n = N_BRANCH + 2 + i
                    if i < 3:
                        lo_split(l, n, n % 2)
                        mix_pair(l, i)
                    else:
                        mix_pair(l, i)
                        lo_split(l, n, n % 2)
                for i in range(4):
                    residual(l, i, N_OUT + i, N_OUT + i, 0.5, l * 8 + (4 + i + 1), cur[:, C_FFN:])
                    n = N_OUT + 2 + i
                    lo_split(l, n, n % 2)
                norm_columns(l * 2 + 2)
                norm_diagonal(l * 2 + 2)
                lo_split(l, N_FFN + 2, 0)
                dve.wait_ge(rstd_ready, l * 2 + 2)
                ffn_gate(l, 0)
                with dve.Fori(1, HT // 2) as j:
                    ffn_hidden(l, j - 1, l * (HT // 2) + j)
                    lo_split(l, N_FFN + 1, 1, j=j)
                    ffn_gate(l, j)
                    lo_split(l, N_FFN + 2, 0, j=j)
                ffn_hidden(l, HT // 2 - 1, l * (HT // 2) + HT // 2)
                for n in range(N_DOWN + 1, STRIPS):
                    i, r = divmod(n - 1 - N_DOWN, 3)
                    if r == 0 and i:
                        residual(l, i - 1, T_DOWN + i - 1, N_DOWN + 3 * i - 1, 1.0, l * 8 + (8 + i),
                                 cur[:, C_NEXT:])
                    lo_split(l, n, n % 2, DOWN_PARTS[(n - N_DOWN) % 3])
                with dve.If(l < DEPTH - 1):
                    lo_split(l, STRIPS, 0)
                residual(l, 3, T_DOWN + 3, STRIPS - 1, 1.0, l * 8 + 12, cur[:, C_NEXT:])
                with dve.If(l < DEPTH - 1):
                    lo_split(l, STRIPS + 1, 1)

            norm_columns(2 * DEPTH + 1, 2 * LAST_ROWS[-1])
            dve.wait_ge(root, 2 * DEPTH + 1)
            for i, tt in ((0, LAST_ROWS[0]), (2, LAST_ROWS[2])):
                dve.wait_ge(y_turned, i + 1)
                nc.vector.tensor_scalar(rows[:, tt, :], psum[:, 2 * tt:2 * tt + 2, :].rearrange("p a b -> p (a b)"),
                                        rcol[:, tt:tt + 1], None, ALU.mult).then_inc(y_dve, 1)


def rotary_tables():
    import numpy as np
    half = HEAD_DIM // 2
    freqs = (10000.0 ** (-np.arange(half, dtype=np.float64) / half)).astype(np.float32)
    ang = (np.arange(SEQ, dtype=np.float32)[None, :] * freqs[:, None]).astype(np.float64)
    c, s = np.cos(ang), np.sin(ang)
    cos = np.concatenate([c, c, c, c])
    sin = np.concatenate([s, -s, s, -s])
    edge = np.array([[1.0 / min(t + 1, 2 << g) for t in range(PAD)] for g in range(N_GROUPS)]).reshape(1, -1)
    return np.concatenate([cos, sin, np.eye(P), np.repeat(edge, P, 0)], axis=1).astype(np.float32)


_INS = ["x", "w_in", "pool_w", "w_branch_pool", "w_branch_attn", "w_gate", "w_out", "w_ffn_gate", "w_ffn_up",
        "w_ffn_down"]


def kernel(**inputs):
    import numpy as _np
    import concourse.bacc as _bacc
    from concourse import mybir as _mybir
    from concourse.bass_utils import run_bass_kernel_spmd as _run

    nc = _bacc.Bacc("TRN2", target_bir_lowering=False, num_devices=1, dynamic_dma_scratch_size=1024)
    arrays, args = {}, []
    for name in _INS:
        a = _np.ascontiguousarray(inputs[name])
        arrays[f"in_{name}_dram"] = a
        args.append(nc.dram_tensor(f"in_{name}_dram", a.shape, _mybir.dt.from_np(a.dtype), kind="ExternalInput").ap())
    v = {n: _np.asarray(inputs[n]) for n in ("norm_mix", "norm_ffn", "norm_final", "b_gate", "pool_scale", "sinks")}
    gains = list(v["norm_mix"]) + [v["norm_final"]]
    per_layer = [_np.concatenate([gains[l + 1], v["norm_ffn"][l], v["b_gate"][l], v["pool_scale"][l]])
                 for l in range(DEPTH)]
    vectors = _np.concatenate(per_layer + [gains[0]]).reshape(C_ALL, P)
    sink_rows = _np.repeat(v["sinks"].reshape(DEPTH, 4, 2).transpose(2, 0, 1), CHUNK, axis=0)
    for name, a in (("vectors", vectors), ("sink_rows", sink_rows), ("tables", rotary_tables())):
        a = _np.ascontiguousarray(a)
        arrays[f"{name}_dram"] = a
        args.append(nc.dram_tensor(f"{name}_dram", a.shape, _mybir.dt.from_np(a.dtype), kind="ExternalInput").ap())
    args.append(nc.dram_tensor("out_dram", (1, SEQ, D_MODEL), _mybir.dt.float32, kind="ExternalOutput").ap())
    trunk(nc, *args)
    r = _run(nc, [arrays], core_ids=[0])
    return r.results[0]["out_dram"]
```

```python
from contextlib import ExitStack

import concourse.bass as bass
from concourse import mybir

P = 128
D_MODEL, SEQ, DEPTH = 1024, 512, 2
CHUNK, HEAD_DIM, EPS = 64, 64, 1e-6
N_GROUPS, PAD = 4, 16
D_FF = 2816
KT = D_MODEL // P
HT = D_FF // P
TT = SEQ // P
STRIP = 2 * P
N_CHUNKS = SEQ // CHUNK

F32 = mybir.dt.float32
F32R = mybir.dt.float32r
ALU = mybir.AluOpType
ACT = mybir.ActivationFunctionType
AX = mybir.AxisListType

N_U, N_KV, N_Q, N_G, N_POOL, N_G7 = 0, 2, 3, 5, 12, 13
N_BRANCH, N_OUT, N_FFN, N_DOWN = 14, 18, 22, 44
STRIPS = N_DOWN + 12
T_DOWN = N_DOWN
TURNS = T_DOWN + 4
DOWN_PARTS = (8, 8, 6)
WARM = 4
WARM_MAIN = 2
IN_ORDER = (0, 1, 4, 2, 3)
Y_BANKS = (0, 1, 4, 5)
LAST_ROWS = (2, 3, 0, 1)


def gate_strip(g):
    return N_G + g if g < 7 else N_G7


C_NEXT, C_FFN, C_BIAS, C_PSCALE, C_LAYER = 0, 8, 16, 32, 36
C_FIRST = DEPTH * C_LAYER
C_ALL = C_FIRST + KT


def trunk(nc, x, w_in, pool_w, w_branch_pool, w_branch_attn, w_gate, w_out, w_ffn_gate, w_ffn_up,
          w_ffn_down, vectors, sink_rows, tables, out):
    ctx = ExitStack()
    with ctx:
        top = [2048]

        def place(name, shape, dt, at=None):
            size = 4
            for s in shape[1:]:
                size *= s
            if at is None:
                at = top[0]
                top[0] += (size + 31) // 32 * 32
            return nc.alloc_sbuf_tensor_at(name, shape, dt, offset=at)

        xT = place("xT", [P, KT, SEQ], F32)
        n_hi = place("n_hi", [P, KT, SEQ], F32R)
        n_lo_at = top[0]
        n_lo = place("n_lo", [P, KT, SEQ], F32R)
        raw = place("raw", [P, 2, KT, STRIP], F32)
        w_hi = place("w_hi", [P, 2, KT, STRIP], F32R)
        w_lo = place("w_lo", [P, 2, KT, STRIP], F32R)
        arena = top[0]
        top[0] += 98304
        gate = place("gate", [P, 2 * KT, SEQ], F32, arena)
        p_hi = place("p_hi", [P, N_GROUPS, SEQ], F32R, arena + 32768)
        p_lo = place("p_lo", [P, N_GROUPS, SEQ], F32R, arena + 40960)
        a_hi = place("a_hi", [P, 4, SEQ], F32R, arena + 49152)
        a_lo = place("a_lo", [P, 4, SEQ], F32R, arena + 57344)
        m_hi = place("m_hi", [P, KT, SEQ], F32R, arena + 65536)
        m_lo = place("m_lo", [P, KT, SEQ], F32R, arena + 81920)
        at = arena + 65536
        qT = place("qT", [P, 4, SEQ], F32, at)
        k_own = place("k_own", [P, SEQ], F32, at + 8192)
        k_swap = place("k_swap", [P, SEQ], F32, at + 10240)
        vT = place("vT", [P, SEQ], F32, at + 12288)
        v_win = place("v_win", [P, N_CHUNKS - 1, P], F32, at + 14336)
        u_pad = place("u_pad", [P, N_GROUPS, PAD + SEQ], F32, at + 17920)
        sum_a = place("sum_a", [P, PAD + SEQ], F32, at + 26368)
        sum_b = place("sum_b", [P, PAD + SEQ], F32, at + 28480)
        cos_r = place("cos_r", [P, SEQ], F32, arena + 49152)
        sin_r = place("sin_r", [P, SEQ], F32, arena + 51200)
        h_hi = place("h_hi", [P, HT, SEQ], F32R, arena)
        h_lo = place("h_lo", [P, HT, SEQ], F32R, arena + 45056)
        gain_diag = nc.alloc_sbuf_tensor_at("gain_diag", [P, KT, P], F32, offset=n_lo_at)
        rows = place("rows", [P, TT, D_MODEL], F32, arena)

        tab = place("tab", [P, 2 * SEQ + P + N_GROUPS * PAD], F32)
        cos, sin = tab[:, 0:SEQ], tab[:, SEQ:2 * SEQ]
        ident = tab[:, 2 * SEQ:2 * SEQ + P]
        edge = tab[:, 2 * SEQ + P:].rearrange("p (g t) -> p g t", g=N_GROUPS)
        rstd = place("rstd", [P, SEQ], F32)
        sumsq = place("sumsq", [P, SEQ], F32)
        work = place("work", [P, 2, SEQ], F32)
        squares = place("squares", [P, 2, SEQ], F32)
        probs = place("probs", [P, 4, P], F32)
        probsT = place("probsT", [P, 4, P], F32)
        ones = place("ones", [P, P], F32)
        vec_rows = place("vec_rows", [C_ALL, P], F32)
        vec = place("vec", [P, C_ALL], F32)
        cur = place("cur", [P, C_LAYER], F32)
        sink_all = place("sink_all", [P, DEPTH, 4], F32)
        sink = place("sink", [P, 4], F32)
        sums_row = place("sums_row", [P, SEQ], F32)
        ms = place("ms", [P, TT], F32)
        inv = place("inv", [P, TT], F32)
        rcol = place("rcol", [P, TT], F32)
        top_s = place("top_s", [P, 4], F32)
        peak = place("peak", [P, 4], F32)
        esink = place("esink", [P, 4], F32)
        total = place("total", [P, 4], F32)
        total_all = place("total_all", [P, 4], F32)
        inv_total = place("inv_total", [P, 4], F32)
        assert top[0] <= nc.sbuf_usable_end

        psum = ctx.enter_context(nc.psum_tensor("psum", [P, 8, SEQ], F32))
        B_S, B_PT, B_O = 4, 6, 7
        B_SUMS = 4

        last_sums_at = psum[:, 2 * LAST_ROWS[1] + 1, 2 * P:2 * P + TT]

        def main(t):
            return psum[:, 2 * (t % 2):2 * (t % 2) + 2, :]

        def side(t):
            return psum[:, 4 + 2 * (t % 2):6 + 2 * (t % 2), :]

        def sem(name):
            return ctx.enter_context(nc.semaphore(name))

        consts_in = sem("consts_in")
        rotary_in = sem("rotary_in")
        gains_ready = sem("gains_ready")
        vec_in = sem("vec_in")
        x_in = [sem(f"x_in{i}") for i in range(KT // 2)]
        sink_in = sem("sink_in")
        out_sent = sem("out_sent")
        raw_landed = [sem("raw_landed0"), sem("raw_landed1")]
        hi_ready = sem("hi_ready")
        lo_ready = sem("lo_ready")
        products = sem("products")
        evacuated = sem("evacuated")
        x_moved = sem("x_moved")
        half_hi = sem("half_hi")
        half_lo = sem("half_lo")
        normed_hi = sem("normed_hi")
        normed_lo = sem("normed_lo")
        squared = sem("squared")
        summed = sem("summed")
        sum_half = sem("sum_half")
        summed_up = sem("summed_up")
        mean_sq = sem("mean_sq")
        inverse = sem("inverse")
        root = sem("root")
        rstd_ready = sem("rstd_ready")
        ones_ready = sem("ones_ready")
        vec_turned = sem("vec_turned")
        vec_ready = sem("vec_ready")
        cur_ready = sem("cur_ready")
        tables_scaled = sem("tables_scaled")
        rotated = sem("rotated")
        pads_clear = sem("pads_clear")
        pool_step = sem("pool_step")
        pooled = sem("pooled")
        pooled_hi = sem("pooled_hi")
        pooled_lo = sem("pooled_lo")
        y_hi = sem("y_hi")
        scores_done = sem("scores_done")
        softmax_step = sem("softmax_step")
        shifted = sem("shifted")
        exps_done = sem("exps_done")
        probs_ready = sem("probs_ready")
        probs_turned = sem("probs_turned")
        probsT_ready = sem("probsT_ready")
        heads_done = sem("heads_done")
        heads_hi = sem("heads_hi")
        heads_lo = sem("heads_lo")
        tanh_done = sem("tanh_done")
        mixed = sem("mixed")
        mix_hi = sem("mix_hi")
        mix_lo = sem("mix_lo")
        silu_done = sem("silu_done")
        hidden = sem("hidden")
        hid_hi = sem("hid_hi")
        hid_lo = sem("hid_lo")
        x_final = sem("x_final")
        y_turned = sem("y_turned")
        y_dve = sem("y_dve")
        y_act = sem("y_act")
        v_turned = sem("v_turned")
        v_ready = sem("v_ready")

        def done(l, n):
            return l * STRIPS + (WARM + n + 1)

        def emptied(l, t):
            return l * TURNS + (WARM_MAIN + t + 1)

        def bank_free(l, t):
            return emptied(l, t - 2)

        def slot_free(l, n):
            return done(l, n - 2)

        def split(l, n):
            return l * STRIPS + (n + 1)

        def raw_free(l, n):
            return split(l, n - 2)

        def half(l, n):
            return l * 2 + {0: 1, N_G7: 2, STRIPS: 3}[n]

        def landed(l, n):
            return l * (32 * (STRIPS // 2)) + 32 * (n // 2 + 1)

        x_cols = x[0].rearrange("(t p) (i c) -> i p t c", p=P, c=STRIP)

        def load_x(eng, i):
            eng.dma_start(rows[:, :, i * STRIP:(i + 1) * STRIP], x_cols[i]).then_inc(x_in[i], 16)

        block = ctx.enter_context(nc.Block())

        @block.sync
        def _(sp):
            def load(l, n, slot, first, second, wait=True):
                if wait:
                    sp.wait_ge(lo_ready, raw_free(l, n))
                for dst, src in (first, second):
                    sp.dma_start(raw[:, slot, dst[0]:dst[1], :], src).then_inc(raw_landed[slot], 16)

            def cols(w, l, c, k0=0, k1=KT, n_k=KT):
                v = w.rearrange("l (k p) m -> l p k m", p=P)
                return v[bass.ds(l, 1), :, k0:k1, bass.ds(c, STRIP)].rearrange("l p k m -> (l p) k m")

            def load_cols(l, n, slot, w, c, at=None, wait=True):
                at = l if at is None else at
                load(l, n, slot, ((0, 4), cols(w, at, c, 0, 4)), ((4, 8), cols(w, at, c, 4, 8)), wait)

            load_x(sp, 0)
            load_cols(0, 0, 0, w_in, IN_ORDER[0] * STRIP, wait=False)
            load_x(sp, 3)
            load_cols(0, 1, 1, w_in, IN_ORDER[1] * STRIP, wait=False)
            with sp.Fori(0, DEPTH) as l:
                for n in range(2, 5):
                    load_cols(l, n, n % 2, w_in, IN_ORDER[n] * STRIP)
                for g in range(7):
                    load_cols(l, gate_strip(g), gate_strip(g) % 2, w_gate, g * STRIP)
                pw = pool_w.rearrange("l (k g) c d -> l c k g d", k=2)[bass.ds(l, 1)].rearrange(
                    "l c k g d -> (l c) k g d")
                sp.wait_ge(lo_ready, raw_free(l, N_POOL))
                for k in range(2):
                    sp.dma_start(raw[:, N_POOL % 2, k, :].rearrange("p (g d) -> p g d", g=2),
                                 pw[:, k]).then_inc(raw_landed[N_POOL % 2], 16)
                load_cols(l, N_G7, N_G7 % 2, w_gate, 7 * STRIP)
                with sp.Fori(0, 2) as i:
                    for s in range(2):
                        c = i * (2 * STRIP) + s * STRIP
                        load(l, i * 2 + (N_BRANCH + s), s,
                             ((0, 4), cols(w_branch_pool, l, c, 0, 4)),
                             ((4, 8), cols(w_branch_attn, l, c, 0, 4)))
                with sp.Fori(0, 2) as i:
                    for s in range(2):
                        load_cols(l, i * 2 + (N_OUT + s), s, w_out, i * (2 * STRIP) + s * STRIP)
                with sp.Fori(0, HT // 2) as j:
                    load_cols(l, j * 2 + N_FFN, 0, w_ffn_gate, j * STRIP)
                    load_cols(l, j * 2 + (N_FFN + 1), 1, w_ffn_up, j * STRIP)
                with sp.Fori(0, 2) as i:
                    for s in range(6):
                        c = i * (2 * STRIP) + (s // 3) * STRIP
                        k0 = sum(DOWN_PARTS[:s % 3])
                        nk = DOWN_PARTS[s % 3]
                        load(l, i * 6 + (N_DOWN + s), s % 2,
                             ((0, nk // 2), cols(w_ffn_down, l, c, k0, k0 + nk // 2)),
                             ((nk // 2, nk), cols(w_ffn_down, l, c, k0 + nk // 2, k0 + nk)))
                with sp.If(l < DEPTH - 1):
                    following = nc.s_assert_within(l + 1, 1, DEPTH - 1, skip_runtime_bounds_check_because=
                                                   "the If above holds only for layers before the last")
                    for n in range(2):
                        load_cols(l, STRIPS + n, n, w_in, IN_ORDER[n] * STRIP, at=following)
            for i, tt in enumerate(LAST_ROWS):
                for h in range(2):
                    if i % 2 == 0:
                        sp.wait_ge(y_dve, i + h + 1)
                    else:
                        sp.wait_ge(y_act, i + h)
                    sp.dma_start(out[0, tt * P:(tt + 1) * P, h * SEQ:(h + 1) * SEQ],
                                 rows[:, tt, h * SEQ:(h + 1) * SEQ]).then_inc(out_sent, 16)
            sp.wait_ge(out_sent, 16 * 2 * TT)

        @block.gpsimd
        def _(pool):
            def sum_squares(count, first, half):
                pool.wait_ge(squared, count)
                if first:
                    nc.gpsimd.tensor_tensor(sumsq[:], squares[:, 0, :], squares[:, 1, :],
                                            ALU.add).then_inc(summed, 1)
                else:
                    pool.wait_ge(summed, count - 1)
                    nc.gpsimd.tensor_tensor(sumsq[:], sumsq[:], squares[:, 0, :],
                                            ALU.add).then_inc(sum_half, 1)
                    pool.wait_ge(sum_half, half)
                    nc.gpsimd.tensor_tensor(sumsq[:], sumsq[:], squares[:, 1, :],
                                            ALU.add).then_inc(summed, 1)
            POOL_STEPS = sum(g + 1 for g in range(N_GROUPS)) + 2 * N_GROUPS

            for i in range(4):
                sum_squares(i + 1, i == 0, i)
            with pool.Fori(0, DEPTH) as l:
                pool.wait_ge(consts_in, 16)
                pool.wait_ge(pads_clear, l + 1)
                step = 0
                for g in range(N_GROUPS):
                    pool.wait_ge(evacuated, emptied(l, N_U + g // 2))
                    u = u_pad[:, g, :]
                    src, bufs = u, [sum_a, sum_b]
                    for e in range(g + 1):
                        d = 1 << e
                        dst = bufs[e % 2]
                        if e:
                            pool.wait_ge(pool_step, l * POOL_STEPS + step)
                        elif g:
                            pool.wait_ge(pooled, l * N_GROUPS + g)
                        nc.gpsimd.tensor_tensor(dst[:, 2 * d - 1:], src[:, 2 * d - 1:],
                                                src[:, d - 1:PAD + SEQ - d], ALU.add).then_inc(pool_step, 1)
                        step += 1
                        src = dst
                    mean = bufs[(g + 1) % 2]
                    pool.wait_ge(pool_step, l * POOL_STEPS + step)
                    nc.gpsimd.tensor_tensor(mean[:, PAD:2 * PAD], src[:, PAD:2 * PAD], edge[:, g, :],
                                            ALU.mult).then_inc(pool_step, 1)
                    nc.gpsimd.tensor_scalar(mean[:, 2 * PAD:], src[:, 2 * PAD:], 1.0 / (2 << g), 1.0,
                                            ALU.mult, ALU.mult).then_inc(pool_step, 1)
                    step += 2
                    pool.wait_ge(pool_step, l * POOL_STEPS + step)
                    nc.gpsimd.tensor_tensor(u[:, PAD:], mean[:, PAD:], u[:, PAD:],
                                            ALU.subtract).then_inc(pooled, 1)
                assert step == POOL_STEPS
                for i in range(7):
                    sum_squares(l * 8 + (4 + i + 1), i % 4 == 0, l * 6 + (3 + i - i // 4))
                with pool.If(l < DEPTH - 1):
                    sum_squares(l * 8 + 12, False, l * 6 + 9)

        @block.scalar
        def _(act):
            act.dma_start(tab[:, 2 * SEQ:], tables[:, 2 * SEQ:]).then_inc(consts_in, 16)
            act.dma_start(vec_rows[:], vectors).then_inc(vec_in, 16)
            for i in (1, 2):
                load_x(act, i)
            act.dma_start(tab[:, 0:2 * SEQ], tables[:, 0:2 * SEQ]).then_inc(rotary_in, 16)
            act.dma_start(sink_all[:], sink_rows).then_inc(sink_in, 16)
            act.wait_ge(ones_ready, 1)
            nc.scalar.activation(probs[:], ones[:].unsqueeze(1).to_broadcast([P, 4, P]), ACT.Copy,
                                 scale=0.0).then_inc(ones_ready, 1)

            def hi_split(l, n, slot, k=KT, j=0, wait=True):
                act.wait_ge(raw_landed[slot], landed(l, n) + 32 * j)
                if wait:
                    act.wait_ge(products, slot_free(l, n) + 2 * j)
                nc.scalar.activation(w_hi[:, slot, 0:k, :], raw[:, slot, 0:k, :], ACT.Copy).then_inc(hi_ready, 1)

            def hi_half(l, n, slot, h, wait=True):
                if h == 0:
                    act.wait_ge(raw_landed[slot], landed(l, n))
                    if wait:
                        act.wait_ge(products, slot_free(l, n))
                k = slice(4 * h, 4 * h + 4)
                nc.scalar.activation(w_hi[:, slot, k, :], raw[:, slot, k, :],
                                     ACT.Copy).then_inc(hi_ready if h else half_hi, 1)

            def square_pair(i, count):
                if count is not None:
                    act.wait_ge(summed, count - 1)
                nc.scalar.activation(squares[:], xT[:, 2 * i:2 * i + 2, :], ACT.Square).then_inc(squared, 1)

            def norm_pair(i, gain):
                for m in (2 * i, 2 * i + 1):
                    nc.scalar.activation(n_hi[:, m, :], xT[:, m, :], ACT.Copy,
                                         scale=gain[:, m:m + 1]).then_inc(normed_hi, 1)

            def norm_root(count):
                act.wait_ge(inverse, count)
                nc.scalar.activation(rstd[:], rstd[:], ACT.Sqrt).then_inc(rstd_ready, 1)

            def first_square(i):
                square_pair(i, i + 1 if i else None)

            def first_norm(i):
                if i < WARM_MAIN:
                    act.wait_ge(evacuated, i + 1)
                else:
                    act.wait_ge(x_moved, i + 1 - WARM_MAIN)
                norm_pair(i, vec[:, C_FIRST:])

            hi_half(0, 0, 0, 0, wait=False)
            first_norm(0)
            hi_half(0, 0, 0, 1)
            first_norm(1)
            first_square(0)
            first_norm(2)
            first_square(1)
            first_norm(3)
            first_square(2)
            hi_split(0, 1, 1, wait=False)
            first_square(3)

            def gate_tanh(l, g):
                act.wait_ge(evacuated, emptied(l, gate_strip(g)))
                for m in (2 * g, 2 * g + 1):
                    nc.scalar.activation(gate[:, m, :], gate[:, m, :], ACT.Tanh, scale=0.5,
                                         bias=cur[:, C_BIAS + m:C_BIAS + m + 1]).then_inc(tanh_done, 1)

            def exps(l, c):
                w = P if c else CHUNK
                act.wait_ge(shifted, l * N_CHUNKS + (c + 1))
                nc.scalar.activation(probs[:, :, 0:w], probs[:, :, 0:w], ACT.Exp).then_inc(exps_done, 1)
                nc.scalar.activation(esink[:], esink[:], ACT.Exp).then_inc(exps_done, 1)

            def move_probsT(l, c):
                act.wait_ge(probs_turned, l * N_CHUNKS + (c + 1))
                nc.scalar.activation(probsT[:], psum[:, B_PT, :].rearrange("p (j r) -> p j r", j=4),
                                     ACT.Copy).then_inc(probsT_ready, 1)

            def move_heads(l, c):
                act.wait_ge(heads_done, l * N_CHUNKS + (c + 1))
                nc.scalar.activation(a_hi[:, :, c * CHUNK:(c + 1) * CHUNK],
                                     psum[:, B_O, 0:4 * CHUNK].rearrange("p (j q) -> p j q", j=4),
                                     ACT.Copy).then_inc(heads_hi, 1)

            def mix_pair(l, i):
                act.wait_ge(mixed, l * 4 + (i + 1))
                nc.scalar.activation(m_hi[:, 2 * i:2 * i + 2, :], work[:], ACT.Copy).then_inc(mix_hi, 1)

            def ffn_gate(l, j):
                act.wait_ge(evacuated, emptied(l, N_FFN) + 2 * j)
                nc.scalar.activation(work[:], work[:], ACT.Silu).then_inc(silu_done, 1)

            def ffn_hidden(l, j, count):
                act.wait_ge(hidden, count)
                nc.scalar.activation(h_hi[:, bass.ds(j * 2, 2), :], squares[:], ACT.Copy).then_inc(hid_hi, 1)

            with act.Fori(0, DEPTH) as l:
                act.wait_ge(cur_ready, l * 2 + 2)
                hi_split(l, 2, 0)
                norm_root(l * 2 + 1)
                for n in range(3, 6):
                    hi_split(l, n, n % 2)
                for w in range(8):
                    if w == 7:
                        for h in range(2):
                            hi_half(l, N_G7, N_G7 % 2, h)
                        for g in range(N_GROUPS):
                            act.wait_ge(products, done(l, N_POOL))
                            nc.scalar.activation(p_hi[:, g, :], psum[:, Y_BANKS[g], :], ACT.Copy,
                                                 scale=cur[:, C_PSCALE + g:C_PSCALE + g + 1]).then_inc(y_hi, 1)
                        hi_split(l, N_BRANCH, 0)
                    if w:
                        move_probsT(l, w - 1)
                    if w < 7:
                        n = gate_strip(w) + 1
                        hi_split(l, n, n % 2, KT if n != N_POOL else 2)
                    if w == 5:
                        act.wait_ge(pooled, l * N_GROUPS + N_GROUPS)
                        nc.scalar.activation(p_hi[:], u_pad[:, :, PAD:], ACT.Copy).then_inc(pooled_hi, 1)
                    if w:
                        gate_tanh(l, w - 1)
                    exps(l, w)
                    if w:
                        move_heads(l, w - 1)
                move_probsT(l, 7)
                hi_split(l, N_BRANCH + 1, 1)
                move_heads(l, 7)
                gate_tanh(l, 7)
                for i in range(4):
                    n = N_BRANCH + 2 + i
                    if i < 3:
                        hi_split(l, n, n % 2)
                        mix_pair(l, i)
                    else:
                        mix_pair(l, i)
                        hi_split(l, n, n % 2)
                for i in range(4):
                    act.wait_ge(evacuated, emptied(l, N_OUT + i))
                    square_pair(i, l * 8 + (4 + i + 1))
                    norm_pair(i, cur[:, C_FFN:])
                    n = N_OUT + 2 + i
                    hi_split(l, n, n % 2)
                hi_split(l, N_FFN + 2, 0)
                norm_root(l * 2 + 2)
                ffn_gate(l, 0)
                with act.Fori(1, HT // 2) as j:
                    ffn_hidden(l, j - 1, l * (HT // 2) + j)
                    hi_split(l, N_FFN + 1, 1, j=j)
                    ffn_gate(l, j)
                    hi_split(l, N_FFN + 2, 0, j=j)
                ffn_hidden(l, HT // 2 - 1, l * (HT // 2) + HT // 2)
                for n in range(N_DOWN + 1, STRIPS):
                    i, r = divmod(n - 1 - N_DOWN, 3)
                    if r == 0 and i:
                        act.wait_ge(evacuated, emptied(l, T_DOWN + i - 1))
                        square_pair(i - 1, l * 8 + (8 + i))
                        with act.If(l < DEPTH - 1):
                            norm_pair(i - 1, cur[:, C_NEXT:])
                    hi_split(l, n, n % 2, DOWN_PARTS[(n - N_DOWN) % 3])
                with act.If(l < DEPTH - 1):
                    for h in range(2):
                        hi_half(l, STRIPS, 0, h)
                with act.If(l < DEPTH - 1):
                    act.wait_ge(evacuated, emptied(l, T_DOWN + 3))
                    square_pair(3, l * 8 + 12)
                    norm_pair(3, cur[:, C_NEXT:])
                    hi_split(l, STRIPS + 1, 1)

            act.wait_ge(summed, 8 * DEPTH + 3)
            for h in range(2):
                act.wait_ge(x_final, h + 1)
                nc.scalar.activation(squares[:, h, :], xT[:, KT - 2 + h, :], ACT.Square).then_inc(squared, 1)
            act.wait_ge(inverse, 2 * DEPTH + 1)
            nc.scalar.activation(rcol[:], inv[:], ACT.Sqrt).then_inc(root, 1)
            act.wait_ge(root, 1)
            for i in (1, 3):
                act.wait_ge(y_turned, i + 1)
                for h in range(2):
                    tt = LAST_ROWS[i]
                    nc.scalar.activation(rows[:, tt, h * SEQ:(h + 1) * SEQ], psum[:, 2 * tt + h, :], ACT.Copy,
                                         scale=rcol[:, tt:tt + 1]).then_inc(y_act, 1)

        @block.tensor
        def _(pe):
            def three(bank, slot, k, m, hi, lo, start, stop):
                c = slice(m * P, (m + 1) * P)
                nc.tensor.matmul(bank, w_lo[:, slot, k, c], hi, start=start, stop=False)
                nc.tensor.matmul(bank, w_hi[:, slot, k, c], lo, start=False, stop=False)
                return nc.tensor.matmul(bank, w_hi[:, slot, k, c], hi, start=False, stop=stop)

            def strip(slot, banks, hi, lo, k0=0, k1=KT, r0=0, before=None, first=True, last=True, end=True):
                for k in range(k0, k1):
                    if before and k in before:
                        before[k]()
                    for m in range(2):
                        mm = three(banks[:, m, :], slot, k, m, hi[:, r0 + k - k0, :], lo[:, r0 + k - k0, :],
                                   first and k == k0, last and k == k1 - 1)
                if end:
                    mm.then_inc(products, 1)

            def ready(l, n, t=None):
                pe.wait_ge(lo_ready, split(l, n))
                if t is not None:
                    pe.wait_ge(evacuated, bank_free(l, t))

            def token_sums(sums):
                pe.wait_ge(summed, sums)
                nc.tensor.matmul(psum[:, B_SUMS, :], ones[:], sumsq[:], start=True, stop=True).then_inc(summed_up, 1)

            def scores_wait(l, c):
                if c == 0:
                    pe.wait_ge(rotated, l * 3 + 3)
                if c == N_CHUNKS - 1:
                    pe.wait_ge(evacuated, emptied(l, N_POOL))
                if c >= 2:
                    pe.wait_ge(shifted, l * N_CHUNKS + (c - 1))

            def scores(l, c):
                k0 = max(c - 1, 0) * CHUNK
                w = (c + 1) * CHUNK - k0
                for j in range(4):
                    for h in range(2):
                        part = slice(h * CHUNK, (h + 1) * CHUNK)
                        keys = k_own if j // 2 == h else k_swap
                        mm = nc.tensor.matmul(psum[part, B_S + c % 2, j * P:j * P + w],
                                              qT[part, j, c * CHUNK:(c + 1) * CHUNK],
                                              keys[part, k0:k0 + w], start=True, stop=True)
                mm.then_inc(scores_done, 1)

            def turn_probs(l, c):
                pe.wait_ge(probs_ready, l * N_CHUNKS + (c + 1))
                if c == 0:
                    pe.wait_ge(v_ready, l + 1)
                for j in range(4):
                    mm = nc.tensor.transpose(psum[:, B_PT, j * P:(j + 1) * P], probs[:, j, :], ident)
                mm.then_inc(probs_turned, 1)

            def heads_wait(l, c):
                pe.wait_ge(probsT_ready, l * N_CHUNKS + (c + 1))
                if c:
                    pe.wait_ge(heads_lo, l * N_CHUNKS + c)

            def heads(l, c):
                keys = slice(0, P if c else CHUNK)
                win = max(c - 1, 0)
                for g in range(2):
                    for h in range(2):
                        o = psum[h * HEAD_DIM:(h + 1) * HEAD_DIM, B_O, g * P:(g + 1) * P]
                        mm = nc.tensor.matmul(o.rearrange("p (j q) -> p j q", j=2),
                                              v_win[keys, win, g * HEAD_DIM:(g + 1) * HEAD_DIM],
                                              probsT[keys, 2 * g:2 * g + 2, h * CHUNK:(h + 1) * CHUNK],
                                              start=True, stop=True)
                mm.then_inc(heads_done, 1)

            def turn_x(tt, m):
                return nc.tensor.matmul(psum[:, 2 * tt + m // 4, (m % 4) * P:(m % 4 + 1) * P],
                                        xT[:, m, tt * P:(tt + 1) * P], gain_diag[:, m, :], start=True, stop=True)

            def last_sums(tile, first=False, last=False):
                for tt in range(TT):
                    mm = nc.tensor.matmul(last_sums_at[:, tt:tt + 1], tile[:, tt * P:(tt + 1) * P], ones[:, 0:1],
                                          start=first and tt == 0, stop=last and tt == TT - 1)
                return mm

            pe.wait_ge(consts_in, 16)
            pe.wait_ge(vec_in, 16)
            nc.tensor.transpose(psum[:, 7, 0:C_ALL], vec_rows[:], ident[0:C_ALL, 0:C_ALL]).then_inc(vec_turned, 1)
            for m in range(KT):
                if m % 2 == 0:
                    pe.wait_ge(x_in[m // 2], 16)
                if m == KT - 1:
                    pe.wait_ge(vec_ready, 1)
                for tt in range(TT):
                    mm = nc.tensor.transpose(psum[:, m, tt * P:(tt + 1) * P], rows[:, tt, m * P:(m + 1) * P],
                                             ident)
                if m % 2:
                    mm.then_inc(products, 1)
            pe.wait_ge(ones_ready, 2)

            with pe.Fori(0, DEPTH) as l:
                def normed(base):
                    return {2 * i: (lambda i=i: pe.wait_ge(normed_lo, l * 8 + (base + i + 1)))
                            for i in range(4)}

                pe.wait_ge(half_lo, half(l, 0))
                pe.wait_ge(evacuated, bank_free(l, 0))
                before = normed(0)
                before[4] = lambda: (pe.wait_ge(normed_lo, l * 8 + 3), pe.wait_ge(lo_ready, split(l, 0)))
                strip(0, main(0), n_hi, n_lo, before=before)
                ready(l, 1, 1)
                strip(1, main(1), n_hi, n_lo, before={2: lambda: token_sums(l * 8 + 4)})
                for n in range(2, N_G):
                    ready(l, n, n)
                    strip(n % 2, main(n), n_hi, n_lo)
                for w in range(8):
                    before = {}
                    if w:
                        before[2] = lambda c=w - 1: turn_probs(l, c)
                        before[5] = lambda c=w - 1: heads_wait(l, c)
                        before[6] = lambda c=w - 1: heads(l, c)
                        before[4] = lambda c=w: scores(l, c)
                    before[7 if w == 0 else 3] = lambda c=w: scores_wait(l, c)
                    if w == 7:
                        ready(l, N_POOL, N_POOL)
                        pe.wait_ge(pooled_lo, l + 1)
                        pe.wait_ge(shifted, l * N_CHUNKS + 7)
                        for g in range(N_GROUPS):
                            mm = three(psum[:, Y_BANKS[g], :], N_POOL % 2, g // 2, g % 2, p_hi[:, g, :],
                                       p_lo[:, g, :], True, True)
                        mm.then_inc(products, 1)
                    n = gate_strip(w)
                    if w < 7:
                        ready(l, n, n)
                    else:
                        pe.wait_ge(half_lo, half(l, n))
                        pe.wait_ge(evacuated, bank_free(l, n))
                        before[3] = lambda: (pe.wait_ge(lo_ready, split(l, N_G7)), scores_wait(l, 7))
                    strip(n % 2, main(n), n_hi, n_lo, before=before)
                    if w == 0:
                        scores(l, 0)
                        for i in range(N_CHUNKS - 1):
                            mm = nc.tensor.transpose(psum[:, B_PT + i // 4, (i % 4) * P:(i % 4 + 1) * P],
                                                     vT[:, i * CHUNK:i * CHUNK + P], ident)
                        mm.then_inc(v_turned, 1)
                for i in range(4):
                    n = N_BRANCH + i
                    ready(l, n, n)
                    before = {0: lambda: turn_probs(l, 7), 1: lambda: heads_wait(l, 7),
                              2: lambda: heads(l, 7)} if i == 0 else None
                    strip(n % 2, main(n), p_hi, p_lo, 0, 4, before=before, end=False)
                    if i == 0:
                        pe.wait_ge(heads_lo, l * N_CHUNKS + N_CHUNKS)
                    strip(n % 2, side(n), a_hi, a_lo, 4, 8)
                with pe.Fori(0, 2) as i:
                    for s in range(2):
                        pe.wait_ge(lo_ready, split(l, N_OUT + s) + 2 * i)
                        pe.wait_ge(evacuated, bank_free(l, N_OUT + s) + 2 * i)
                        before = {2 * q: (lambda q=q: pe.wait_ge(mix_lo, l * 4 + (q + 1))) for q in range(4)}
                        strip(s, main(s), m_hi, m_lo, before=before)

                def ffn(j, stats=None):
                    for s in range(2):
                        pe.wait_ge(lo_ready, split(l, N_FFN + s) + 2 * j)
                        pe.wait_ge(evacuated, bank_free(l, N_FFN + s) + 2 * j)
                        before = None
                        if stats:
                            before = normed(4) if s == 0 else {2: lambda: token_sums(l * 8 + 8)}
                        strip(s, main(s), n_hi, n_lo, before=before)

                ffn(0, True)
                with pe.Fori(1, HT // 2) as j:
                    ffn(j)
                with pe.Fori(0, 2) as i:
                    for s in range(6):
                        r = s % 3
                        if s == 4:
                            with pe.If(l * 2 + i > 2 * DEPTH - 2):
                                pe.wait_ge(gains_ready, 1)
                                pe.wait_ge(evacuated, emptied(DEPTH - 1, TURNS - 2))
                                for m in range(6):
                                    for tt in LAST_ROWS[0:2]:
                                        turn_x(tt, m)
                                pe.wait_ge(summed, 8 * DEPTH + 3)
                                last_sums(sumsq[:], first=True)
                        pe.wait_ge(lo_ready, split(l, N_DOWN + s) + 6 * i)
                        if r == 0:
                            pe.wait_ge(evacuated, bank_free(l, T_DOWN + s // 3) + 2 * i)
                        if r < 2:
                            pe.wait_ge(hid_lo, l * (HT // 2) + 4 * (r + 1))
                            before = None
                        else:
                            pe.wait_ge(hid_lo, l * (HT // 2) + (HT // 2 - 1))
                            before = {DOWN_PARTS[2] - 2: lambda: pe.wait_ge(hid_lo, l * (HT // 2) + HT // 2)}
                        strip(s % 2, main(s // 3), h_hi, h_lo, 0, DOWN_PARTS[r], sum(DOWN_PARTS[:r]),
                              before=before, first=r == 0, last=r == 2)

            def turn_tiles(tt, m0, m1):
                for m in range(m0, m1):
                    mm = turn_x(tt, m)
                return mm
            t0, t1, t2, t3 = LAST_ROWS
            turn_tiles(t2, 0, 6)
            pe.wait_ge(squared, 8 * DEPTH + 4)
            last_sums(squares[:, 0, :])
            pe.wait_ge(squared, 8 * DEPTH + 5)
            last_sums(squares[:, 1, :], last=True).then_inc(summed_up, 1)
            pe.wait_ge(x_final, 2)
            turn_tiles(t0, 6, 8).then_inc(y_turned, 1)
            pe.wait_ge(mean_sq, 2 * DEPTH + 1)
            turn_tiles(t1, 6, 8).then_inc(y_turned, 1)
            turn_tiles(t2, 6, 8).then_inc(y_turned, 1)
            turn_tiles(t3, 0, KT).then_inc(y_turned, 1)

        @block.vector
        def _(dve):
            nc.vector.memset(ones[:], 1.0).then_inc(ones_ready, 1)

            def lo_split(l, n, slot, k=KT, j=0):
                dve.wait_ge(hi_ready, l * STRIPS + (n + 1) + 2 * j)
                nc.vector.tensor_tensor(w_lo[:, slot, 0:k, :], raw[:, slot, 0:k, :],
                                        w_hi[:, slot, 0:k, :].bitcast(F32), ALU.subtract).then_inc(lo_ready, 1)

            def lo_half(l, n, slot, h):
                if h:
                    dve.wait_ge(hi_ready, split(l, n))
                else:
                    dve.wait_ge(half_hi, half(l, n))
                k = slice(4 * h, 4 * h + 4)
                nc.vector.tensor_tensor(w_lo[:, slot, k, :], raw[:, slot, k, :], w_hi[:, slot, k, :].bitcast(F32),
                                        ALU.subtract).then_inc(lo_ready if h else half_lo, 1)

            def norm_pair(i, count, gain):
                for m in (2 * i, 2 * i + 1):
                    dve.wait_ge(normed_hi, count * 2 - (2 * i + 1 - m))
                    mm = nc.vector.scalar_tensor_tensor(n_lo[:, m, :], xT[:, m, :], gain[:, m:m + 1],
                                                        n_hi[:, m, :].bitcast(F32), ALU.mult, ALU.subtract)
                mm.then_inc(normed_lo, 1)

            def norm_inverse(count, sums, ms, inv):
                dve.wait_ge(summed_up, count)
                nc.vector.tensor_scalar(ms, sums, 1.0 / D_MODEL, EPS, ALU.mult, ALU.add).then_inc(mean_sq, 1)
                dve.wait_ge(mean_sq, count)
                nc.vector.reciprocal(inv, ms).then_inc(inverse, 1)

            def pair(ap):
                return ap.unsqueeze(1).to_broadcast([P, 2, SEQ])

            dve.wait_ge(vec_turned, 1)
            nc.vector.tensor_copy(vec[:], psum[:, 7, 0:C_ALL]).then_inc(vec_ready, 1)
            dve.wait_ge(vec_ready, 1)
            bias = vec[:, 0:C_FIRST].rearrange("p (l c) -> p l c", l=DEPTH)[:, :, C_BIAS:C_PSCALE]
            nc.vector.tensor_scalar(bias, bias, 0.5, None, ALU.mult).then_inc(vec_ready, 1)

            def move_x(i):
                dve.wait_ge(products, i + 1)
                mm = nc.vector.tensor_copy(xT[:, 2 * i:2 * i + 2, :], psum[:, 2 * i:2 * i + 2, :])
                if i < WARM_MAIN:
                    mm.then_inc(evacuated, 1)
                else:
                    mm.then_inc(x_moved, 1)

            def first_norm(i):
                if i < WARM_MAIN:
                    dve.wait_ge(evacuated, i + 1)
                else:
                    dve.wait_ge(x_moved, i + 1 - WARM_MAIN)
                norm_pair(i, i + 1, vec[:, C_FIRST:])

            move_x(0)
            move_x(1)
            lo_half(0, 0, 0, 0)
            first_norm(0)
            move_x(2)
            first_norm(1)
            lo_half(0, 0, 0, 1)
            first_norm(2)
            move_x(3)
            first_norm(3)
            lo_split(0, 1, 1)
            dve.wait_ge(consts_in, 16)
            dve.wait_ge(rotary_in, 16)
            dve.wait_ge(sink_in, 16)
            dve.wait_ge(vec_ready, 2)

            def rotate(l, t, n_rot, dsts, count):
                src = main(t)[:, 0:n_rot, :]
                by = [P, n_rot, SEQ]
                if t > N_KV:
                    dve.wait_ge(rotated, count - 1)
                nc.vector.tensor_tensor(work[:, 0:n_rot, :], src, cos_r[:].unsqueeze(1).to_broadcast(by), ALU.mult)
                for q in range(4):
                    a, b = q * 32, (q ^ 1) * 32
                    mm = nc.vector.tensor_tensor(
                        squares[a:a + 32, 0:n_rot, :], src[b:b + 32],
                        sin_r[b:b + 32, :].unsqueeze(1).to_broadcast([32, n_rot, SEQ]), ALU.mult)
                mm.then_inc(evacuated, 1)
                dve.wait_ge(evacuated, emptied(l, t))
                for dst, part in dsts:
                    mm = nc.vector.tensor_tensor(dst, work[part, 0:n_rot, :], squares[part, 0:n_rot, :], ALU.add)
                mm.then_inc(rotated, 1)

            STEPS = 5

            def shift_scores(l, c):
                w = P if c else CHUNK
                s = psum[:, B_S + c % 2, :].rearrange("p (j k) -> p j k", j=4)[:, :, 0:w]
                at = l * (STEPS * N_CHUNKS) + STEPS * c
                dve.wait_ge(scores_done, l * N_CHUNKS + (c + 1))
                nc.vector.tensor_reduce(top_s[:], s, AX.X, ALU.max).then_inc(softmax_step, 1)
                dve.wait_ge(softmax_step, at + 1)
                nc.vector.scalar_tensor_tensor(peak[:], top_s[:], HEAD_DIM ** -0.5, sink[:], ALU.mult,
                                               ALU.max).then_inc(softmax_step, 1)
                dve.wait_ge(softmax_step, at + 2)
                nc.vector.tensor_tensor(esink[:], sink[:], peak[:], ALU.subtract)
                if c:
                    dve.wait_ge(probs_turned, l * N_CHUNKS + c)
                nc.vector.scalar_tensor_tensor(probs[:, :, 0:w], s, HEAD_DIM ** -0.5,
                                               peak[:].unsqueeze(2).to_broadcast([P, 4, w]), ALU.mult,
                                               ALU.subtract).then_inc(shifted, 1)

            def normalise(l, c):
                w = P if c else CHUNK
                at = l * (STEPS * N_CHUNKS) + STEPS * c
                dve.wait_ge(exps_done, l * (2 * N_CHUNKS) + 2 * (c + 1))
                nc.vector.tensor_reduce(total[:], probs[:, :, 0:w], AX.X, ALU.add).then_inc(softmax_step, 1)
                dve.wait_ge(softmax_step, at + 3)
                nc.vector.tensor_tensor(total_all[:], total[:], esink[:], ALU.add).then_inc(softmax_step, 1)
                dve.wait_ge(softmax_step, at + 4)
                nc.vector.reciprocal(inv_total[:], total_all[:]).then_inc(softmax_step, 1)
                dve.wait_ge(softmax_step, at + 5)
                nc.vector.tensor_tensor(probs[:, :, 0:w], probs[:, :, 0:w],
                                        inv_total[:].unsqueeze(2).to_broadcast([P, 4, w]),
                                        ALU.mult).then_inc(probs_ready, 1)

            def move_heads(l, c):
                dve.wait_ge(heads_hi, l * N_CHUNKS + (c + 1))
                cols = slice(c * CHUNK, (c + 1) * CHUNK)
                nc.vector.tensor_tensor(a_lo[:, :, cols],
                                        psum[:, B_O, 0:4 * CHUNK].rearrange("p (j q) -> p j q", j=4),
                                        a_hi[:, :, cols].bitcast(F32), ALU.subtract).then_inc(heads_lo, 1)

            def scaled(l, t, dst):
                dve.wait_ge(products, done(l, t))
                nc.vector.tensor_tensor(dst, main(t), pair(rstd[:]), ALU.mult).then_inc(evacuated, 1)

            def mix_pair(l, i):
                t = N_BRANCH + i
                if i == 0:
                    dve.wait_ge(tanh_done, l * 16 + 16)
                else:
                    dve.wait_ge(mix_lo, l * 4 + i)
                dve.wait_ge(products, done(l, t))
                nc.vector.scalar_tensor_tensor(work[:], gate[:, 2 * i:2 * i + 2, :], 1.0, main(t), ALU.add,
                                               ALU.mult)
                nc.vector.scalar_tensor_tensor(squares[:], gate[:, KT + 2 * i:KT + 2 * i + 2, :], 1.0,
                                               side(t), ALU.add, ALU.mult).then_inc(evacuated, 1)
                dve.wait_ge(evacuated, emptied(l, t))
                nc.vector.tensor_tensor(work[:], work[:], squares[:], ALU.add).then_inc(mixed, 1)
                dve.wait_ge(mix_hi, l * 4 + (i + 1))
                dve.wait_ge(mixed, l * 4 + (i + 1))
                nc.vector.tensor_tensor(m_lo[:, 2 * i:2 * i + 2, :], work[:],
                                        m_hi[:, 2 * i:2 * i + 2, :].bitcast(F32), ALU.subtract).then_inc(mix_lo, 1)

            def residual(l, i, t, n, factor):
                dve.wait_ge(products, done(l, n))
                tiles = xT[:, 2 * i:2 * i + 2, :]
                nc.vector.scalar_tensor_tensor(tiles, main(t), factor, tiles, ALU.mult,
                                               ALU.add).then_inc(evacuated, 1)

            def down_residual(l, i):
                residual(l, i, T_DOWN + i, N_DOWN + 3 * i + 2, 1.0)

            def next_norm(l, i):
                dve.wait_ge(evacuated, emptied(l, T_DOWN + i))
                norm_pair(i, l * 8 + (8 + i + 1), cur[:, C_NEXT:])

            def ffn_gate(l, j):
                dve.wait_ge(products, done(l, N_FFN) + 2 * j)
                nc.vector.tensor_tensor(work[:], main(N_FFN), pair(rstd[:]), ALU.mult).then_inc(evacuated, 1)

            def ffn_hidden(l, j, count):
                dve.wait_ge(lo_ready, split(l, N_FFN + 2) + 2 * j)
                dve.wait_ge(products, done(l, N_FFN + 1) + 2 * j)
                nc.vector.tensor_tensor(squares[:], main(N_FFN + 1), pair(rstd[:]), ALU.mult).then_inc(evacuated, 1)
                dve.wait_ge(evacuated, emptied(l, N_FFN + 1) + 2 * j)
                dve.wait_ge(silu_done, count)
                nc.vector.tensor_tensor(squares[:], squares[:], work[:], ALU.mult).then_inc(hidden, 1)
                dve.wait_ge(hidden, count)
                dve.wait_ge(hid_hi, count)
                tiles = bass.ds(j * 2, 2)
                nc.vector.tensor_tensor(h_lo[:, tiles, :], squares[:], h_hi[:, tiles, :].bitcast(F32),
                                        ALU.subtract).then_inc(hid_lo, 1)

            with dve.Fori(0, DEPTH) as l:
                dve.wait_ge(normed_lo, l * 8 + 4)
                nc.vector.tensor_copy(cur[:], vec[:, bass.ds(l * C_LAYER, C_LAYER)]).then_inc(cur_ready, 1)
                nc.vector.tensor_copy(sink[:], sink_all[:, bass.ds(l, 1), :].rearrange("p a j -> p (a j)")
                                      ).then_inc(cur_ready, 1)
                nc.vector.memset(u_pad[:, :, 0:PAD], 0.0).then_inc(pads_clear, 1)
                dve.wait_ge(cur_ready, l * 2 + 2)
                lo_split(l, 2, 0)
                norm_inverse(l * 2 + 1, psum[:, B_SUMS, :], sums_row[:], rstd[:])
                dve.wait_ge(rstd_ready, l * 2 + 1)
                scaled(l, N_U, u_pad[:, 0:2, PAD:])
                nc.vector.tensor_tensor(cos_r[:], cos, rstd[:], ALU.mult)
                nc.vector.tensor_tensor(sin_r[:], sin, rstd[:], ALU.mult).then_inc(tables_scaled, 1)
                lo_split(l, 3, 1)
                scaled(l, N_U + 1, u_pad[:, 2:4, PAD:])
                dve.wait_ge(tables_scaled, l + 1)
                dve.wait_ge(products, done(l, N_KV))
                nc.vector.tensor_tensor(vT[:], main(N_KV)[:, 1, :], rstd[:], ALU.mult)
                lower, upper = slice(0, HEAD_DIM), slice(HEAD_DIM, P)
                rotate(l, N_KV, 1, [(k_own[:].unsqueeze(1), slice(0, P)),
                                    (k_swap[upper, :].unsqueeze(1), lower),
                                    (k_swap[lower, :].unsqueeze(1), upper)],
                       l * 3 + 1)
                lo_split(l, 4, 0)
                dve.wait_ge(products, done(l, N_Q))
                rotate(l, N_Q, 2, [(qT[:, 0:2, :], slice(0, P))], l * 3 + 2)
                lo_split(l, 5, 1)
                for w in range(8):
                    def split_next():
                        if w < 7:
                            n = gate_strip(w) + 1
                            lo_split(l, n, n % 2, KT if n != N_POOL else 2)
                        else:
                            for h in range(2):
                                lo_half(l, N_G7, N_G7 % 2, h)
                    if w == 0:
                        dve.wait_ge(products, done(l, N_Q + 1))
                        rotate(l, N_Q + 1, 2, [(qT[:, 2:4, :], slice(0, P))], l * 3 + 3)
                        split_next()
                    else:
                        g = w - 1
                        scaled(l, gate_strip(g), gate[:, 2 * g:2 * g + 2, :])
                        split_next()
                    if w == 7:
                        for g in range(N_GROUPS):
                            dve.wait_ge(y_hi, l * N_GROUPS + (g + 1))
                            mm = nc.vector.scalar_tensor_tensor(p_lo[:, g, :], psum[:, Y_BANKS[g], :],
                                                                cur[:, C_PSCALE + g:C_PSCALE + g + 1],
                                                                p_hi[:, g, :].bitcast(F32), ALU.mult, ALU.subtract)
                        mm.then_inc(evacuated, 1)
                        lo_split(l, N_BRANCH, 0)
                    if w == 5:
                        dve.wait_ge(pooled_hi, l + 1)
                        nc.vector.tensor_tensor(p_lo[:], u_pad[:, :, PAD:], p_hi[:].bitcast(F32),
                                                ALU.subtract).then_inc(pooled_lo, 1)
                    shift_scores(l, w)
                    if w == 0:
                        dve.wait_ge(v_turned, l + 1)
                        flat = psum[:, B_PT:B_O + 1, :].rearrange("p a b -> p (a b)")[:, 0:(N_CHUNKS - 1) * P]
                        nc.vector.tensor_copy(v_win[:].rearrange("p a b -> p (a b)"), flat).then_inc(v_ready, 1)
                    normalise(l, w)
                    if w:
                        move_heads(l, w - 1)
                scaled(l, N_G7, gate[:, 14:16, :])
                move_heads(l, 7)
                lo_split(l, N_BRANCH + 1, 1)
                for i in range(4):
                    n = N_BRANCH + 2 + i
                    if i < 3:
                        lo_split(l, n, n % 2)
                        mix_pair(l, i)
                    else:
                        mix_pair(l, i)
                        lo_split(l, n, n % 2)
                for i in range(4):
                    residual(l, i, N_OUT + i, N_OUT + i, 0.5)
                    dve.wait_ge(evacuated, emptied(l, N_OUT + i))
                    norm_pair(i, l * 8 + (4 + i + 1), cur[:, C_FFN:])
                    n = N_OUT + 2 + i
                    lo_split(l, n, n % 2)
                lo_split(l, N_FFN + 2, 0)
                norm_inverse(l * 2 + 2, psum[:, B_SUMS, :], sums_row[:], rstd[:])
                dve.wait_ge(rstd_ready, l * 2 + 2)
                ffn_gate(l, 0)
                with dve.Fori(1, HT // 2) as j:
                    ffn_hidden(l, j - 1, l * (HT // 2) + j)
                    lo_split(l, N_FFN + 1, 1, j=j)
                    ffn_gate(l, j)
                    lo_split(l, N_FFN + 2, 0, j=j)
                ffn_hidden(l, HT // 2 - 1, l * (HT // 2) + HT // 2)
                for n in range(N_DOWN + 1, STRIPS):
                    i, r = divmod(n - 1 - N_DOWN, 3)
                    if r == 0 and i:
                        down_residual(l, i - 1)
                        with dve.If(l < DEPTH - 1):
                            next_norm(l, i - 1)
                        if i == 1:
                            with dve.If(l > DEPTH - 2):
                                gains = cur[:, C_NEXT:C_NEXT + KT].unsqueeze(2).to_broadcast([P, KT, P])
                                nc.vector.tensor_tensor(gain_diag[:], ident.unsqueeze(1).to_broadcast([P, KT, P]),
                                                        gains, ALU.mult).then_inc(gains_ready, 1)
                    lo_split(l, n, n % 2, DOWN_PARTS[(n - N_DOWN) % 3])
                with dve.If(l < DEPTH - 1):
                    for h in range(2):
                        lo_half(l, STRIPS, 0, h)
                    down_residual(l, 3)
                    next_norm(l, 3)
                    lo_split(l, STRIPS + 1, 1)

            dve.wait_ge(products, done(DEPTH - 1, STRIPS - 1))
            for h in range(2):
                tile = xT[:, KT - 2 + h, :]
                nc.vector.tensor_tensor(tile, main(TURNS - 1)[:, h, :], tile, ALU.add).then_inc(x_final, 1)

            norm_inverse(2 * DEPTH + 1, last_sums_at, ms[:], inv[:])
            dve.wait_ge(root, 1)
            for i in (0, 2):
                dve.wait_ge(y_turned, i + 1)
                for h in range(2):
                    tt = LAST_ROWS[i]
                    nc.vector.tensor_scalar(rows[:, tt, h * SEQ:(h + 1) * SEQ], psum[:, 2 * tt + h, :],
                                            rcol[:, tt:tt + 1], None, ALU.mult).then_inc(y_dve, 1)


def rotary_tables():
    import numpy as np
    half = HEAD_DIM // 2
    freqs = (10000.0 ** (-np.arange(half, dtype=np.float64) / half)).astype(np.float32)
    ang = (np.arange(SEQ, dtype=np.float32)[None, :] * freqs[:, None]).astype(np.float64)
    c, s = np.cos(ang), np.sin(ang)
    cos = np.concatenate([c, c, c, c])
    sin = np.concatenate([s, -s, s, -s])
    edge = np.array([[1.0 / min(t + 1, 2 << g) for t in range(PAD)] for g in range(N_GROUPS)]).reshape(1, -1)
    return np.concatenate([cos, sin, np.eye(P), np.repeat(edge, P, 0)], axis=1).astype(np.float32)


_INS = ["x", "w_in", "pool_w", "w_branch_pool", "w_branch_attn", "w_gate", "w_out", "w_ffn_gate", "w_ffn_up",
        "w_ffn_down"]


def kernel(**inputs):
    import numpy as _np
    import concourse.bacc as _bacc
    from concourse import mybir as _mybir
    from concourse.bass_utils import run_bass_kernel_spmd as _run

    nc = _bacc.Bacc("TRN2", target_bir_lowering=False, num_devices=1, dynamic_dma_scratch_size=1024)
    arrays, args = {}, []
    for name in _INS:
        a = _np.ascontiguousarray(inputs[name])
        arrays[f"in_{name}_dram"] = a
        args.append(nc.dram_tensor(f"in_{name}_dram", a.shape, _mybir.dt.from_np(a.dtype), kind="ExternalInput").ap())
    v = {n: _np.asarray(inputs[n]) for n in ("norm_mix", "norm_ffn", "norm_final", "b_gate", "pool_scale", "sinks")}
    gains = list(v["norm_mix"]) + [v["norm_final"]]
    per_layer = [_np.concatenate([gains[l + 1], v["norm_ffn"][l], v["b_gate"][l], v["pool_scale"][l]])
                 for l in range(DEPTH)]
    vectors = _np.concatenate(per_layer + [gains[0]]).reshape(C_ALL, P)
    sink_rows = _np.repeat(v["sinks"].reshape(DEPTH, 4, 2).transpose(2, 0, 1), CHUNK, axis=0)
    for name, a in (("vectors", vectors), ("sink_rows", sink_rows), ("tables", rotary_tables())):
        a = _np.ascontiguousarray(a)
        arrays[f"{name}_dram"] = a
        args.append(nc.dram_tensor(f"{name}_dram", a.shape, _mybir.dt.from_np(a.dtype), kind="ExternalInput").ap())
    args.append(nc.dram_tensor("out_dram", (1, SEQ, D_MODEL), _mybir.dt.float32, kind="ExternalOutput").ap())
    trunk(nc, *args)
    r = _run(nc, [arrays], core_ids=[0])
    return r.results[0]["out_dram"]
```
